# Optimizing a Trainium2 kernel written in Bass

```python
import functools
import jax
import jax.numpy as jnp
from jax import lax
import numpy as np

D_MODEL = 1024
BATCH = 1
SEQ = 1024
DEPTH = 1
DEC_BATCH = 8
DEC_SEQ = 4
PAST_LEN = 8192
PAGE_SIZE = 128

D_MIX = D_MODEL
D_ATTN = D_MIX // 2
D_CONV = D_MIX - D_ATTN
HEAD_DIM = 64
N_HEADS = D_ATTN // HEAD_DIM
N_KV_HEADS = 2
GROUP = N_HEADS // N_KV_HEADS
KV_DIM = N_KV_HEADS * HEAD_DIM
WINDOW = 128
ATTN_BLOCK = WINDOW
WIN_BUF = min(WINDOW, PAST_LEN)
CONV_W = 3
IN_SPLITS = (D_ATTN, D_ATTN + KV_DIM, D_ATTN + 2 * KV_DIM,
             D_ATTN + 2 * KV_DIM + D_CONV, D_ATTN + 2 * KV_DIM + 2 * D_CONV)
IN_COLS = D_ATTN + 2 * KV_DIM + 3 * D_CONV
N_ADA = 6
PEER_HEADS = 8
N_KEYS = 128
N_EXPERTS = N_KEYS * N_KEYS
PEER_TOPK = 16
D_KEY = 256
D_HALF = D_KEY // 2
PEER_BLOCK = 256
EPS = 1e-6
NEG_INF = -1e30

kernel_name = 'hymba_conv_swa_peer_step'

def rmsnorm(x, g):
    xf = x.astype(jnp.float32)
    y = xf * lax.rsqrt(jnp.mean(xf * xf, axis=-1, keepdims=True) + EPS)
    return (y * g.astype(jnp.float32)).astype(x.dtype)

def alibi_slopes():
    h = jnp.arange(1, N_HEADS + 1, dtype=jnp.float32)
    return jnp.exp2(-8.0 * h / N_HEADS).reshape(N_KV_HEADS, GROUP)

def attn_core(q, k, v, dist, valid, sinks):
    s = jnp.einsum('nbqkgd,nbskd->nbkgqs', q, k, preferred_element_type=jnp.float32) * (HEAD_DIM ** -0.5)
    s = s - alibi_slopes()[:, :, None, None] * dist[:, None, None]
    s = jnp.where(valid[:, None, None], s, NEG_INF)
    sink = sinks.astype(jnp.float32).reshape(N_KV_HEADS, GROUP)[:, :, None, None]
    m = jnp.maximum(jnp.max(s, axis=-1, keepdims=True), sink)
    p = jnp.exp(s - m)
    w = p / (jnp.sum(p, axis=-1, keepdims=True) + jnp.exp(sink - m))
    o = jnp.einsum('nbkgqs,nbskd->nbqkgd', w, v.astype(jnp.float32))
    return o.astype(q.dtype)

def window_attention_prompt(q, k, v, sinks):
    b, s = q.shape[:2]
    nb = s // ATTN_BLOCK
    qb = q.reshape(b, nb, ATTN_BLOCK, N_KV_HEADS, GROUP, HEAD_DIM)

    def band(t):
        tb = t.reshape(b, nb, ATTN_BLOCK, N_KV_HEADS, HEAD_DIM)
        prev = jnp.pad(tb, ((0, 0), (1, 0), (0, 0), (0, 0), (0, 0)))[:, :-1]
        return jnp.concatenate([prev, tb], axis=2)

    blk = jnp.arange(nb)[:, None, None]
    qpos = blk * ATTN_BLOCK + jnp.arange(ATTN_BLOCK)[None, :, None]
    kpos = (blk - 1) * ATTN_BLOCK + jnp.arange(2 * ATTN_BLOCK)[None, None, :]
    d = qpos - kpos
    valid = (d >= 0) & (d < WINDOW) & (kpos >= 0)
    o = attn_core(qb, band(k), band(v), d.astype(jnp.float32), valid, sinks)
    return o.reshape(b, s, D_ATTN)

def prompt_attend(q, k, v, sinks):
    return window_attention_prompt(q, k, v, sinks), k[:, -WIN_BUF:], v[:, -WIN_BUF:]

def sample_attend(q, k, v, k_buf, v_buf, sinks):
    n, t = q.shape[:2]
    k_all = jnp.concatenate([k_buf.astype(k.dtype), k], axis=1)
    v_all = jnp.concatenate([v_buf.astype(v.dtype), v], axis=1)
    qpos = PAST_LEN + jnp.arange(t)
    kpos = jnp.concatenate([PAST_LEN - WIN_BUF + jnp.arange(WIN_BUF), qpos])
    d = qpos[:, None] - kpos[None, :]
    valid = (d >= 0) & (d < WINDOW) & (kpos[None, :] >= 0)
    o = attn_core(q.reshape(n, 1, t, N_KV_HEADS, GROUP, HEAD_DIM), k_all[:, None], v_all[:, None],
                  d[None].astype(jnp.float32), valid[None], sinks)
    return o.reshape(n, t, D_ATTN), k_all[:, -WIN_BUF:], v_all[:, -WIN_BUF:]

def short_conv(u, prev, w):
    t = u.shape[1]
    up = jnp.concatenate([prev.astype(u.dtype), u], axis=1)
    y = w[0] * up[:, 0:t]
    for j in range(1, CONV_W):
        y = y + w[j] * up[:, j:j + t]
    return y, up[:, -(CONV_W - 1):]

def peer_ffn(h, wq, keys, u_tab, v_tab):
    shape = h.shape
    xt = h.reshape(-1, shape[-1])
    n_tok = xt.shape[0]
    pad = (-n_tok) % PEER_BLOCK
    xb = jnp.pad(xt, ((0, pad), (0, 0))).reshape(-1, PEER_BLOCK, shape[-1])
    n_cand = PEER_TOPK * PEER_TOPK

    def block(xblk):
        q = (xblk @ wq).reshape(PEER_BLOCK, PEER_HEADS, 2, D_HALF)
        sc = jnp.einsum('thpc,hpnc->thpn', q, keys, preferred_element_type=jnp.float32)
        s_top, i_top = lax.top_k(sc, PEER_TOPK)
        cand = (s_top[:, :, 0, :, None] + s_top[:, :, 1, None, :]).reshape(PEER_BLOCK, PEER_HEADS, n_cand)
        cand_idx = (i_top[:, :, 0, :, None] * N_KEYS + i_top[:, :, 1, None, :]).reshape(PEER_BLOCK, PEER_HEADS, n_cand)
        best, pos = lax.top_k(cand, PEER_TOPK)
        experts = jnp.take_along_axis(cand_idx, pos, axis=-1)
        gates = jax.nn.softmax(best, axis=-1)
        act = jax.nn.gelu(jnp.einsum('thkd,td->thk', u_tab[experts], xblk,
                                     preferred_element_type=jnp.float32), approximate=False)
        return jnp.einsum('thk,thkd->td', (gates * act).astype(v_tab.dtype), v_tab[experts])

    y = lax.map(block, xb).reshape(-1, shape[-1])[:n_tok]
    return y.reshape(shape).astype(h.dtype)

def decoder_layer(x, c, conv_prev, attend, norm_mix_g, norm_ffn_g, w_ada, b_ada, w_in, conv_w, w_out,
                  peer_wq, peer_keys, peer_u, peer_v):
    n, t = x.shape[:2]
    mod = jax.nn.silu(c) @ w_ada + b_ada
    sh1, sc1, g1, sh2, sc2, g2 = [m[:, None, :] for m in jnp.split(mod, N_ADA, axis=-1)]
    h = rmsnorm(x, norm_mix_g) * (1 + sc1) + sh1
    q, k, v, bg, cg, hc = jnp.split(h @ w_in, IN_SPLITS, axis=-1)
    z_attn, k_state, v_state = attend(q.reshape(n, t, N_HEADS, HEAD_DIM),
                                      k.reshape(n, t, N_KV_HEADS, HEAD_DIM),
                                      v.reshape(n, t, N_KV_HEADS, HEAD_DIM))
    z_conv, conv_state = short_conv(cg * hc, conv_prev, conv_w)
    z_conv = bg * z_conv
    x = x + g1 * (jnp.concatenate([z_attn, z_conv], axis=-1) @ w_out)
    h2 = rmsnorm(x, norm_ffn_g) * (1 + sc2) + sh2
    x = x + g2 * peer_ffn(h2, peer_wq, peer_keys, peer_u, peer_v)
    return x, k_state, v_state, conv_state

def setup_inputs(seed: int = 0) -> dict:
    key = jax.random.key(seed)
    ks = jax.random.split(key, 20)

    def nrm(k, shape, scale):
        return jax.random.normal(k, shape, jnp.float32) * scale

    return {
        'x_prompt': nrm(ks[0], (BATCH, SEQ, D_MODEL), 1.0),
        'x_sample': nrm(ks[1], (DEC_BATCH, DEC_SEQ, D_MODEL), 1.0),
        'c_prompt': nrm(ks[2], (BATCH, D_MODEL), 1.0),
        'c_sample': nrm(ks[3], (DEC_BATCH, D_MODEL), 1.0),
        'cache_k': nrm(ks[4], (DEPTH, DEC_BATCH, WIN_BUF, N_KV_HEADS, HEAD_DIM), 1.0),
        'cache_v': nrm(ks[5], (DEPTH, DEC_BATCH, WIN_BUF, N_KV_HEADS, HEAD_DIM), 1.0),
        'state_conv': nrm(ks[6], (DEPTH, DEC_BATCH, CONV_W - 1, D_CONV), 1.0),
        'norm_mix_g': 1.0 + nrm(ks[7], (DEPTH, D_MODEL), 0.05),
        'norm_ffn_g': 1.0 + nrm(ks[8], (DEPTH, D_MODEL), 0.05),
        'w_ada': nrm(ks[9], (DEPTH, D_MODEL, N_ADA * D_MODEL), 0.5 * D_MODEL ** -0.5),
        'b_ada': nrm(ks[10], (DEPTH, N_ADA * D_MODEL), 0.01),
        'w_in': nrm(ks[11], (DEPTH, D_MODEL, IN_COLS), D_MODEL ** -0.5),
        'conv_w': nrm(ks[12], (DEPTH, CONV_W, D_CONV), CONV_W ** -0.5),
        'attn_sinks': nrm(ks[13], (DEPTH, N_HEADS), 1.0),
        'w_out': nrm(ks[14], (DEPTH, D_MIX, D_MODEL), D_MIX ** -0.5),
        'peer_wq': nrm(ks[15], (DEPTH, D_MODEL, PEER_HEADS * D_KEY), D_MODEL ** -0.5),
        'peer_keys': nrm(ks[16], (DEPTH, PEER_HEADS, 2, N_KEYS, D_HALF), D_HALF ** -0.5),
        'peer_u': nrm(ks[17], (DEPTH, N_EXPERTS, D_MODEL), D_MODEL ** -0.5),
        'peer_v': nrm(ks[18], (DEPTH, N_EXPERTS, D_MODEL), 1.0),
        'norm_final_g': 1.0 + nrm(ks[19], (D_MODEL,), 0.05),
    }

def reference(x_prompt, x_sample, c_prompt, c_sample, cache_k, cache_v, state_conv,
              norm_mix_g, norm_ffn_g, w_ada, b_ada, w_in, conv_w, attn_sinks, w_out,
              peer_wq, peer_keys, peer_u, peer_v, norm_final_g):
    yp, ys = x_prompt, x_sample
    kp_l, vp_l, cp_l, ks_l, vs_l, cs_l = [], [], [], [], [], []
    for l in range(DEPTH):
        weights = (norm_mix_g[l], norm_ffn_g[l], w_ada[l], b_ada[l], w_in[l], conv_w[l], w_out[l],
                   peer_wq[l], peer_keys[l], peer_u[l], peer_v[l])
        att_p = functools.partial(prompt_attend, sinks=attn_sinks[l])
        att_s = functools.partial(sample_attend, k_buf=cache_k[l], v_buf=cache_v[l], sinks=attn_sinks[l])
        conv0 = jnp.zeros((yp.shape[0], CONV_W - 1, D_CONV), yp.dtype)
        yp, kp, vp, cp = decoder_layer(yp, c_prompt, conv0, att_p, *weights)
        ys, kss, vss, css = decoder_layer(ys, c_sample, state_conv[l], att_s, *weights)
        kp_l.append(kp); vp_l.append(vp); cp_l.append(cp)
        ks_l.append(kss); vs_l.append(vss); cs_l.append(css)
    yp = rmsnorm(yp, norm_final_g)
    ys = rmsnorm(ys, norm_final_g)
    return (yp, ys, jnp.stack(kp_l), jnp.stack(vp_l), jnp.stack(cp_l),
            jnp.stack(ks_l), jnp.stack(vs_l), jnp.stack(cs_l))


_drawn_inputs = setup_inputs


def setup_inputs(seed=0):
    import zlib

    import numpy as np

    out = dict(_drawn_inputs(seed))
    spreads = {}
    factors = {'attn_sinks': 4.31}
    for name, (base, spread) in spreads.items():
        noise = np.random.default_rng([zlib.crc32(name.encode()), seed]).standard_normal(out[name].shape)
        drawn = base * np.exp(spread * noise) if base else spread * noise
        out[name] = jnp.asarray(drawn.astype(out[name].dtype))
    for name, factor in factors.items():
        out[name] = (out[name] * factor).astype(out[name].dtype)
    return out
```

```python
from contextlib import ExitStack

import numpy as np

import concourse.bass as bass
from concourse import mybir

D = 1024
KT = D // 128
SEQ, NS, TS = 1024, 8, 4
NSAMP = NS * TS
T = SEQ + NSAMP
PT = SEQ // 128
TT = PT + 1
TH = T // 3
DH, NH, NKV = 64, 8, 2
GRP = NH // NKV
WIN = 128
DC = 512
CT = DC // 128
INC = 512 + 256 + 3 * DC
NADA = 6
PH, NK, TOPK = 8, 128, 16
CAND = TOPK * TOPK
UNITS = 2 + PT * PH
EPS = 1e-6
NEG = -1e30
LOW = -3.0e38
BATCH = 4
NB = TOPK // BATCH

f32 = mybir.dt.float32
i32 = mybir.dt.int32
u32 = mybir.dt.uint32
ALU = mybir.AluOpType
ACT = mybir.ActivationFunctionType
AX = mybir.AxisListType


def rows_of(t):
    return 128 if t < PT else NSAMP


def build(nc, a, out):
    ctx = ExitStack()
    with ctx:
        def sb(name, shape, dt=f32):
            return ctx.enter_context(nc.sbuf_tensor(name, shape, dt))

        def sem(name):
            return ctx.enter_context(nc.semaphore(name))

        mod_d = nc.dram_tensor("mod_d", (1 + NS, NADA * D), f32, kind="Internal").ap()
        x1_d = nc.dram_tensor("x1_d", (T, D), f32, kind="Internal").ap()
        h2_d = nc.dram_tensor("h2_d", (T, D), f32, kind="Internal").ap()
        sc_d = nc.dram_tensor("sc_d", (UNITS + 2, 128, 2 * NK), f32, kind="Internal").ap()

        arena = sb("arena", [128, 51600])

        def R(off, *shape, p=128):
            n = int(np.prod(shape))
            v = arena[0:p, off:off + n]
            if len(shape) == 2:
                v = v.rearrange("p (a b) -> p a b", a=shape[0])
            if len(shape) == 3:
                v = v.rearrange("p (a b c) -> p a b c", a=shape[0], b=shape[1])
            return v

        hT = R(0, KT, T)
        crow, cexp = R(0, D, p=9), R(1024, D, p=9)
        wada = [R(8448, KT, 512), R(12544, KT, 512)]
        modrow = R(16896, NADA * D, p=9)
        brow = R(23232, NADA * D, p=9)
        zT = R(8448, KT, T)
        qT = R(16896, 4, T)
        kT, vT = R(21120, T), R(22176, T)
        bT = R(23232, CT, T)
        uP = R(27456, CT, SEQ + 2)
        uS = R(31560, CT, NS, TS + 2)
        cgT = R(31752, CT, T)
        vnat = R(35976, TT, 128)
        A1s, B1s = R(35976, D, p=NSAMP), R(37000, D, p=NSAMP)
        gmix = R(38024, D)
        cKn, cKT, cVn = R(37128, NS, 128), R(38152, NS, 128), R(39176, NS, 128)
        win = [R(40200 + 1024 * i, KT, 128) for i in range(4)]
        biasP = R(40200, NH, 256)
        biasS = R(42248, NKV, NS * 160, p=16)
        xin = [R(44808 + 1024 * i, D) for i in range(2)]
        hbuf = [R(46856 + 1024 * i, D) for i in range(2)]
        sqj = R(31752, D)
        S = [R(44808 + 1024 * i, GRP, 256) for i in range(2)]
        PTb = [R(46856 + 1024 * i, 2, 512) for i in range(2)]
        SS = R(44808, NS, 160, p=16)
        PTc, PTn = R(46856, NS, 16), R(46984, NS, 16, p=NSAMP)
        A1, B1 = R(48904, D), R(49928, D)
        kn7, kn8 = R(48904, 128), R(49032, 128, p=NSAMP)
        utP, utS = R(49160, DC, p=2), R(49672, DC, p=16)
        stn = R(50952, DC, p=16)
        wout = R(0, KT, D)
        h2T = R(16896, KT, T)
        vec = [R(25344 + 1024 * i, D) for i in range(3)]
        vecs = [R(28416 + 1024 * i, D, p=NSAMP) for i in range(3)]
        x4 = [R(31752 + 1024 * i, D) for i in range(2)]
        x1b = [R(33800 + 1024 * i, D) for i in range(2)]
        h2b = [R(35848 + 1024 * i, D) for i in range(2)]
        sqj4 = R(37896, D)
        gffn = R(38920, D)
        wq = [R(8448 + 1024 * i, KT, 128) for i in range(8)]
        keysN, keysT = R(40200, 2 * PH, 128), R(42248, 2 * PH, 128)
        qTc = [R(44808 + T * i, T) for i in range(2)]
        scE = [R(46920 + 2048 * i, PT, 256) for i in range(2)]
        qS = R(51016, 2 * PH, NSAMP)
        scS = R(37896, 2, 256)
        Ur = R(0, TOPK, D)
        Vr = R(16384, TOPK, D)
        scb = [R(32768 + 256 * i, 2, NK) for i in range(2)]
        h2c, x1c, Y, g2v, gfv = (R(33280 + 1024 * i, D) for i in range(5))
        dotj = R(38400, D)
        diag = [R(39424 + 2048 * i, TOPK, 128) for i in range(2)]
        x2b, yb = R(43520, D), R(44544, D)
        g2s = R(45568, D, p=NSAMP)
        cand, cand2, cidx1 = R(46592, TOPK, TOPK), R(46848, CAND), R(47104, 128)
        oh, oh2 = R(47232, TOPK, TOPK), R(47488, TOPK, TOPK)
        sc2 = R(47744, 2, NK)
        sqj6 = R(48256, D)

        ident, sel = sb("ident", [128, 128]), sb("sel", [128, NSAMP])
        iota = sb("iota", [128, TOPK])
        sink = sb("sink", [128, NH])
        cw = sb("cw", [128, 3, CT])
        utail = sb("utail", [128, CT, 16])
        q16 = sb("q16", [128, NS, 16])
        cwn = sb("cwn", [3 * CT, 128])
        cT = sb("cT", [128, KT, 9])
        ss, rinv = sb("ss", [128, 2]), sb("rinv", [128, 2])
        mx, negm, esk, rs = (sb(n, [128, 2, 4]) for n in ("mx", "negm", "esk", "rs"))
        smx, sden = sb("smx", [16, NS]), sb("sden", [16, NS])
        ses = sb("ses", [16, NS])
        topv = sb("topv", [128, 2, TOPK])
        topi = sb("topi", [128, 2, TOPK], u32)
        topf = sb("topf", [128, 2, TOPK])
        best = sb("best", [128, 2, TOPK])
        nbest = sb("nbest", [128, 2, 1])
        pos = sb("pos", [128, TOPK], u32)
        posx = sb("posx", [128, 2, TOPK], u32)
        posf = sb("posf", [128, 2, TOPK])
        ef = sb("ef", [128, 2, TOPK])
        eid = [sb(f"eid{i}", [128, TOPK], i32) for i in range(2)]
        gex, gsum = sb("gex", [128, 2, TOPK]), sb("gsum", [128, 2])
        grec = sb("grec", [128, 2])
        act = sb("act", [128, 2, TOPK])
        gel = sb("gel", [128, 2, TOPK])
        wgt = sb("wgt", [128, 2, TOPK])
        rin, epsb = sb("rin", [128, 5]), sb("epsb", [128, 1])
        tickv = sb("tickv", [128, 4])
        sinkS = sb("sinkS", [16, NKV])
        PS = ctx.enter_context(nc.psum_tensor("PS", [128, 8, 512], f32))

        names = """const_ld cexp_done csil_done ct_ps ct_done pe_mod mod_ev mod_st vec1_ld ss_done h_done
            pe_hT hT_ev pe_p2 p2_evA p2_evD state_ld cache_ld pe_b b_ev bias_ld pe_sc S_done m_done e_done
            p_done pe_pt pt_ev pe_pv z_ev z_conv sss_done sm_done se_done sp_done spt_ps spt_ev spv_ps
            wout_ld vec4_ld pe_o x1_done ss4_done h2_done pe_h2T h2T_ev keys_ld pe_k k_ev pe_q q_ev pe_s
            sc_ev scs_ev pe_ss pad_st scs_st h2_ld x1_ld vec6_ld idx_ready exp_done dots_done gelu_done w_ready
            diag_ready pv_done y_added y_sum fin_ss y_out y_st pe_sel out_st g1_ld h2s_ld ticked
            pool_turn""".split()
        s = {n: sem(n) for n in names}
        wada_ld = [sem(f"wada_ld{i}") for i in range(2)]
        x_ld = [sem(f"x_ld{i}") for i in range(2)]
        win_ld = [sem(f"win_ld{i}") for i in range(4)]
        x4_ld = [sem(f"x4_ld{i}") for i in range(2)]
        x1_st = [sem(f"x1_st{i}") for i in range(2)]
        wq_ld = [sem(f"wq_ld{i}") for i in range(8)]
        sc_st = [sem(f"sc_st{i}") for i in range(2)]
        sc_ld = [sem(f"sc_ld{i}") for i in range(2)]
        u_ld = [sem(f"u_ld{i}") for i in range(NB)]
        v_ld = [sem(f"v_ld{i}") for i in range(NB)]

        block = ctx.enter_context(nc.Block())
        NCONST = 16

        def x_rows(t):
            return a["x_prompt"][t * 128:(t + 1) * 128, :] if t < PT else a["x_sample"]

        def in_cols(ct):
            return [(ct * 64, 64), (256 + ct * 64, 64)] if ct < 4 else [(ct * 128, 128)]

        @block.sync
        def _(sp):
            for dst, src in ((ident[:, :], a["ident"]), (sel[:, :], a["sel"]), (iota[:, :], a["iota"]),
                             (sink[:, :], a["attn_sinks"].partition_broadcast(128)),
                             (crow[0:1, :], a["c_prompt"]), (crow[1:9, :], a["c_sample"]),
                             (brow, a["b_ada"].partition_broadcast(9))):
                sp.dma_start(dst, src).then_inc(s["const_ld"], 16)
            for kv in range(NKV):
                for i in range(GRP):
                    h = kv * GRP + i
                    sp.dma_start(sinkS[i * TS:(i + 1) * TS, kv:kv + 1],
                                 a["attn_sinks"][h:h + 1].partition_broadcast(TS)).then_inc(s["const_ld"], 16)
            sp.dma_start(cwn[:, :], a["conv_w"].rearrange("j (c p) -> (j c) p", p=128)).then_inc(s["const_ld"], 16)
            wv = a["w_ada"].rearrange("(k p) c -> p k c", p=128)
            for g in range(12):
                if g >= 2:
                    sp.wait_ge(s["pe_mod"], g - 1)
                sp.dma_start(wada[g % 2], wv[:, :, g * 512:(g + 1) * 512]).then_inc(wada_ld[g % 2], 16)
            wv2 = a["w_in"].rearrange("(k p) c -> p k c", p=128)
            for ct in range(18):
                if ct >= 4:
                    sp.wait_ge(s["pe_p2"], ct - 3)
                n = 0
                for c0, w in in_cols(ct):
                    sp.dma_start(win[ct % 4][:, :, n:n + w], wv2[:, :, c0:c0 + w]).then_inc(win_ld[ct % 4], 16)
                    n += w
            sp.wait_ge(s["pe_p2"], 18)
            sp.dma_start(biasP, a["alibi_p"]).then_inc(s["bias_ld"], 16)
            sp.dma_start(biasS, a["alibi_s"]).then_inc(s["bias_ld"], 16)
            for kv in range(NKV):
                sp.dma_start(wout[kv * 64:(kv + 1) * 64, 0:4, :],
                             a["w_out"][kv * 256:(kv + 1) * 256, :].rearrange("(i d) c -> d i c", d=64)).then_inc(s["wout_ld"], 16)
            sp.dma_start(wout[:, 4:8, :], a["w_out"][512:1024, :].rearrange("(k p) c -> p k c", p=128)).then_inc(s["wout_ld"], 16)
            sp.wait_ge(s["z_conv"], 1)
            for t in range(TT + 1):
                if t < TT:
                    r = rows_of(t)
                    if t >= 2:
                        sp.wait_ge(s["x1_done"], t - 1)
                    sp.dma_start(x4[t % 2][0:r, :], x_rows(t)).then_inc(x4_ld[t % 2], 16)
                if t >= 1:
                    r = rows_of(t - 1)
                    sp.wait_ge(s["x1_done"], t)
                    sp.dma_start(x1_d[(t - 1) * 128:(t - 1) * 128 + r, :], x1b[(t - 1) % 2][0:r, :]).then_inc(x1_st[(t - 1) % 2], 16)
                    sp.wait_ge(s["h2_done"], t)
                    sp.dma_start(h2_d[(t - 1) * 128:(t - 1) * 128 + r, :], h2b[(t - 1) % 2][0:r, :]).then_inc(x1_st[(t - 1) % 2], 16)
            wqv = a["peer_wq"].rearrange("(k p) c -> p k c", p=128)
            sp.wait_ge(s["pe_o"], TT)
            sp.wait_ge(s["p_done"], 16)
            sp.wait_ge(s["sp_done"], NKV)
            sp.dma_start(keysN, a["peer_keys"].rearrange("h q n c -> n (h q) c")).then_inc(s["keys_ld"], 16)
            for c in range(2 * PH):
                if c >= 8:
                    sp.wait_ge(s["pe_q"], c - 7)
                sp.dma_start(wq[c % 8], wqv[:, :, c * 128:(c + 1) * 128]).then_inc(wq_ld[c % 8], 16)
            for h in range(PH):
                sp.wait_ge(s["sc_ev"], 2 * h + 2)
                sp.dma_start(sc_d[2 + h:2 + h + PT * PH - PH + 1:PH, :, :].rearrange("u t c -> t u c"), scE[h % 2]).then_inc(sc_st[h % 2], 16)
            sp.wait_ge(s["scs_ev"], 1)
            for u0 in (0, UNITS):
                sp.dma_start(sc_d[u0:u0 + 2, :, :].rearrange("u t c -> t u c"), scS).then_inc(s["scs_st"], 16)
            sp.wait_ge(s["scs_st"], 32)
            for i in range(2):
                sp.wait_ge(sc_st[i], 64)
                sp.wait_ge(x1_st[i], 16 * (10 if i == 0 else 8))

            for i in range(2):
                sp.dma_start(scb[i], sc_d[i, :, :].rearrange("t (a b) -> t a b", a=2)).then_inc(sc_ld[i], 16)
            for qd in range(4):
                sp.dma_start(h2c[qd * 32:(qd + 1) * 32, :], h2_d[SEQ:T, :]).then_inc(s["h2s_ld"], 16)
            sp.dma_start(x1c[0:NSAMP, :], x1_d[SEQ:T, :]).then_inc(s["x1_ld"], 16)
            sp.dma_start(g2v, mod_d[0, 5 * D:6 * D].partition_broadcast(128)).then_inc(s["vec6_ld"], 16)
            sp.dma_start(gfv, a["norm_final_g"].partition_broadcast(128)).then_inc(s["vec6_ld"], 16)
            for j in range(TS):
                sp.dma_start(g2s[j:NSAMP:TS, :], mod_d[1:9, 5 * D:6 * D]).then_inc(s["vec6_ld"], 16)
            for i in range(2):
                sp.wait_ge(s["idx_ready"], i + 1)
                sp.dma_start(scb[i], sc_d[i + 2, :, :].rearrange("t (a b) -> t a b", a=2)).then_inc(sc_ld[i], 16)
            sp.wait_ge(s["y_out"], 1)
            sp.dma_start(out["y_sample"], yb[0:NSAMP, :]).then_inc(s["out_st"], 16)
            with sp.Fori(0, PT) as t:
                sp.wait_ge(s["dots_done"], t * (PH * NB) + 2 * NB)
                sp.dma_start(h2c, h2_d[bass.ds(t * 128, 128), :]).then_inc(s["h2_ld"], 16)
                sp.wait_ge(s["y_out"], t + 1)
                sp.dma_start(x1c, x1_d[bass.ds(t * 128, 128), :]).then_inc(s["x1_ld"], 16)
                for u in range(PH):
                    sp.wait_ge(s["idx_ready"], t * PH + (u + 3))
                    sp.dma_start(scb[u % 2], sc_d[bass.ds(t * PH + (u + 4), 1), :, :]
                                 .rearrange("u t (a b) -> (u t) a b", a=2)).then_inc(sc_ld[u % 2], 16)
                sp.wait_ge(s["y_out"], t + 2)
                sp.dma_start(out["y_prompt"][bass.ds(t * 128, 128), :], yb).then_inc(s["out_st"], 16)
            sp.wait_ge(s["out_st"], 16 * TT)
            for i in range(2):
                sp.wait_ge(sc_ld[i], 16 * (PT * PH // 2 + 2))
            sp.wait_ge(s["g1_ld"], 16 * (6 + 2 * NS))

        @block.gpsimd
        def _(po):
            po.dma_start(stn, a["state_conv"]).then_inc(s["state_ld"], 16)
            po.wait_ge(s["mod_ev"], 4)
            po.dma_start(mod_d[:, 0:2 * D], modrow[:, 0:2 * D]).then_inc(s["mod_st"], 16)
            po.dma_start(gmix, a["norm_mix_g"].partition_broadcast(128)).then_inc(s["vec1_ld"], 16)
            po.wait_ge(s["mod_st"], 16)
            for dst, dsts, part in ((B1, B1s, 0), (A1, A1s, 1)):
                po.dma_start(dst, mod_d[0, part * D:(part + 1) * D].partition_broadcast(128)).then_inc(s["vec1_ld"], 16)
                for j in range(TS):
                    po.dma_start(dsts[j:NSAMP:TS, :], mod_d[1:9, part * D:(part + 1) * D]).then_inc(s["vec1_ld"], 16)
            po.wait_ge(s["mod_ev"], 12)
            po.dma_start(mod_d[:, 2 * D:6 * D], modrow[:, 2 * D:6 * D]).then_inc(s["mod_st"], 16)
            po.wait_ge(s["h_done"], TT)
            po.dma_start(cKn, a["cache_k"].rearrange("n s c -> s n c")).then_inc(s["cache_ld"], 16)
            po.dma_start(cVn, a["cache_v"].rearrange("n s c -> s n c")).then_inc(s["cache_ld"], 16)
            for name, src in (("k_sample", "cache_k"), ("v_sample", "cache_v")):
                po.dma_start(out[name][:, 0:WIN - TS, :], a[src][:, TS:WIN, :]).then_inc(s["g1_ld"], 16)
            po.wait_ge(s["b_ev"], 8)
            po.dma_start(out["k_prompt"], kn7).then_inc(s["g1_ld"], 16)
            po.dma_start(out["v_prompt"], vnat[:, PT - 1, :]).then_inc(s["g1_ld"], 16)
            po.dma_start(out["conv_prompt"], utP).then_inc(s["g1_ld"], 16)
            po.dma_start(out["conv_sample"], utS).then_inc(s["g1_ld"], 16)
            for n in range(NS):
                po.dma_start(out["k_sample"][n, WIN - TS:WIN, :], kn8[n * TS:(n + 1) * TS, :]).then_inc(s["g1_ld"], 16)
                po.dma_start(out["v_sample"][n, WIN - TS:WIN, :], vnat[n * TS:(n + 1) * TS, PT, :]).then_inc(s["g1_ld"], 16)
            po.wait_ge(s["z_conv"], 1)
            po.wait_ge(s["mod_st"], 32)
            for i, part in enumerate((2, 4, 3)):
                po.dma_start(vec[i], mod_d[0, part * D:(part + 1) * D].partition_broadcast(128)).then_inc(s["vec4_ld"], 16)
                for j in range(TS):
                    po.dma_start(vecs[i][j:NSAMP:TS, :], mod_d[1:9, part * D:(part + 1) * D]).then_inc(s["vec4_ld"], 16)
            po.wait_ge(s["pe_pv"], 16)
            po.wait_ge(s["spv_ps"], NKV)
            po.dma_start(gffn, a["norm_ffn_g"].partition_broadcast(128)).then_inc(s["vec4_ld"], 16)
            po.wait_ge(s["pe_ss"], 1)
            for i in range(2):
                po.wait_ge(x1_st[i], 16 * (10 if i == 0 else 8))

            def gathers(m, first):
                par, mm = m
                for table, ring, landed, used in (("peer_u", Ur, u_ld, "dots_done"), ("peer_v", Vr, v_ld, "pv_done")):
                    for b in range(NB):
                        if table == "peer_u" and b == 0:
                            po.wait_ge(s["idx_ready"], mm + 1)
                        if not first:
                            po.wait_ge(s[used], mm * NB + (b + 1 - NB))
                        if not isinstance(mm, int):
                            po.sem_inc(s["pool_turn"], 1)
                        for k in range(b * BATCH, (b + 1) * BATCH):
                            po.indirect_dma_start(
                                out=ring[:, k, :], out_offset=None, in_=a[table],
                                in_offset=bass.IndirectOffsetOnAxis(ap=eid[par][:, k:k + 1], axis=0),
                            ).then_inc(landed[b], 16)

            gathers((0, 0), True)
            gathers((1, 1), False)
            with po.Fori(0, PT) as t:
                for u in range(PH):
                    gathers((u % 2, t * PH + (u + 2)), False)

        @block.tensor
        def _(pe):
            mm = pe.matmul
            pe.wait_ge(s["const_ld"], 16 * NCONST)
            pe.wait_ge(s["csil_done"], 1)
            for k in range(KT):
                last = pe.transpose(PS[:, 0, k * 9:(k + 1) * 9], crow[:, k * 128:(k + 1) * 128], ident[0:9, 0:9])
            last = pe.transpose(PS[:, 0, 72:72 + 3 * CT], cwn[:, :], ident[0:3 * CT, 0:3 * CT])
            last.then_inc(s["ct_ps"], 1)
            pe.wait_ge(s["ct_done"], 1)
            for g in range(12):
                pe.wait_ge(wada_ld[g % 2], 16 * (g // 2 + 1))
                if g >= 2:
                    pe.wait_ge(s["mod_ev"], g - 1)
                for k in range(KT):
                    last = mm(PS[0:9, 1 + g % 2, :], cT[:, k, :], wada[g % 2][:, k, :], start=k == 0, stop=k == KT - 1)
                last.then_inc(s["pe_mod"], 1)
            for t in range(TT):
                r = rows_of(t)
                pe.wait_ge(s["h_done"], t + 1)
                if t >= 2:
                    pe.wait_ge(s["hT_ev"], t - 1)
                b = 3 + 2 * (t % 2)
                for k in range(KT):
                    last = pe.transpose(PS[:, b + k // 4, (k % 4) * r:(k % 4 + 1) * r],
                                        hbuf[t % 2][0:r, k * 128:(k + 1) * 128], ident[0:r, 0:r])
                last.then_inc(s["pe_hT"], 1)
            pe.wait_ge(s["hT_ev"], TT)
            for ct in range(18):
                pe.wait_ge(win_ld[ct % 4], 16 * sum(len(in_cols(c)) for c in range(ct % 4, ct + 1, 4)))
                if ct >= 2:
                    if ct - 2 < 14:
                        pe.wait_ge(s["p2_evA"], ct - 1)
                    else:
                        pe.wait_ge(s["p2_evD"], ct - 15)
                for j in range(3):
                    for k in range(KT):
                        last = mm(PS[:, 3 * (ct % 2) + j, 0:TH], win[ct % 4][:, k, :], hT[:, k, j * TH:(j + 1) * TH],
                                  start=k == 0, stop=k == KT - 1)
                last.then_inc(s["pe_p2"], 1)
            for t in range(PT):
                last = pe.transpose(PS[:, 6 + t // 4, (t % 4) * 128:(t % 4 + 1) * 128], vT[:, t * 128:(t + 1) * 128], ident[:, :])
                if t % 4 == 3:
                    last.then_inc(s["pe_b"], 1)
            pe.wait_ge(s["p2_evD"], 4)
            pe.transpose(PS[0:NSAMP, 0, 0:128], vT[:, SEQ:T], ident[:, :])
            pe.transpose(PS[0:NSAMP, 0, 128:256], kT[:, SEQ:T], ident[:, :])
            pe.transpose(PS[:, 0, 256:384], kT[:, SEQ - 128:SEQ], ident[:, :]).then_inc(s["pe_b"], 1)
            pe.wait_ge(s["state_ld"], 16)
            for c in range(CT):
                last = pe.transpose(PS[:, 1, c * 16:(c + 1) * 16], stn[:, c * 128:(c + 1) * 128], ident[0:16, 0:16])
            last.then_inc(s["pe_b"], 1)
            pe.wait_ge(s["cache_ld"], 32)
            for n in range(NS):
                last = pe.transpose(PS[:, 4 + n // 4, (n % 4) * 128:(n % 4 + 1) * 128], cKn[:, n, :], ident[:, :])
                if n % 4 == 3:
                    last.then_inc(s["pe_b"], 1)
            pe.wait_ge(s["b_ev"], 1)
            for c in range(CT):
                last = pe.transpose(PS[0:2, 2, c * 128:(c + 1) * 128], uP[:, c, SEQ:SEQ + 2], ident[:, :])
            last.then_inc(s["pe_b"], 1)
            for c in range(CT):
                last = pe.transpose(PS[0:16, 3, c * 128:(c + 1) * 128], utail[:, c, :], ident[:, :])
            last.then_inc(s["pe_b"], 1)
            pe.wait_ge(s["b_ev"], 8)

            def scores(n):
                blk, kv = n // 2, n % 2
                p, lo = kv * 64, 128 if blk == 0 else 0
                if n >= 2:
                    pe.wait_ge(s["S_done"], n - 1)
                for i in range(GRP):
                    last = mm(PS[:, 2 * (n % 2) + i // 2, (i % 2) * 256 + lo:(i % 2 + 1) * 256],
                              qT[p:p + 64, i, blk * 128:(blk + 1) * 128],
                              kT[p:p + 64, (blk - 1) * 128 + lo:(blk + 1) * 128], start=True, stop=True)
                last.then_inc(s["pe_sc"], 1)

            def values(n):
                blk, kv = n // 2, n % 2
                p = kv * 64
                pe.wait_ge(s["pt_ev"], n + 1)
                if kv == 0 and blk >= 2:
                    pe.wait_ge(s["z_ev"], blk - 1)
                for half in ((1,) if blk == 0 else (0, 1)):
                    last = mm(PS[p:p + 64, 6 + blk % 2, :], vnat[:, blk - 1 + half, p:p + 64], PTb[n % 2][:, half, :],
                              start=half == (1 if blk == 0 else 0), stop=half == 1)
                last.then_inc(s["pe_pv"], 1)

            scores(0)
            for n in range(2 * PT):
                if n + 1 < 2 * PT:
                    scores(n + 1)
                pe.wait_ge(s["p_done"], n + 1)
                if n >= 1:
                    pe.wait_ge(s["pt_ev"], n)
                for half in ((1,) if n < 2 else (0, 1)):
                    for i in range(GRP):
                        last = pe.transpose(PS[:, 4 + half, i * 128:(i + 1) * 128], S[n % 2][:, i, half * 128:(half + 1) * 128], ident[:, :])
                last.then_inc(s["pe_pt"], 1)
                if n >= 1:
                    values(n - 1)
            values(2 * PT - 1)
            pe.wait_ge(s["S_done"], 2 * PT)
            for kv in range(NKV):
                p = kv * 64
                if kv:
                    pe.wait_ge(s["sss_done"], 1)
                for n in range(NS):
                    q = q16[p:p + 64, n, :]
                    mm(PS[0:16, n // 4, (n % 4) * 128:(n % 4 + 1) * 128], q, cKT[p:p + 64, n, :], start=True, stop=True)
                    last = mm(PS[0:16, 2, n * 32:(n + 1) * 32], q, kT[p:p + 64, SEQ:T], start=True, stop=True)
                last.then_inc(s["pe_sc"], 1)
                pe.wait_ge(s["sp_done"], kv + 1)
                pe.wait_ge(s["pt_ev"], 2 * PT)
                if kv:
                    pe.wait_ge(s["spt_ev"], 1)
                for n in range(NS):
                    pe.transpose(PS[:, 4, n * 16:(n + 1) * 16], SS[:, n, 0:128], ident[0:16, 0:16])
                    last = pe.transpose(PS[0:NSAMP, 5, n * 16:(n + 1) * 16], SS[:, n, 128:160], ident[0:16, 0:16])
                last.then_inc(s["spt_ps"], 1)
                pe.wait_ge(s["spt_ev"], kv + 1)
                if kv == 0:
                    pe.wait_ge(s["z_ev"], PT - 1)
                for n in range(NS):
                    mm(PS[p:p + 64, 6, n * 16:(n + 1) * 16], cVn[:, n, p:p + 64], PTc[:, n, :], start=True, stop=False)
                    last = mm(PS[p:p + 64, 6, n * 16:(n + 1) * 16], vnat[0:NSAMP, PT, p:p + 64], PTn[:, n, :], start=False, stop=True)
                last.then_inc(s["spv_ps"], 1)

            pe.wait_ge(s["wout_ld"], 48)
            pe.wait_ge(s["z_ev"], PT + 1)
            pe.wait_ge(s["z_conv"], 1)

            def project(t):
                r = rows_of(t)
                if t >= 2:
                    pe.wait_ge(s["x1_done"], t - 1)
                for half in range(2):
                    for k in range(KT):
                        last = mm(PS[0:r, 2 * (t % 2) + half, :], zT[:, k, t * 128:t * 128 + r], wout[:, k, half * 512:(half + 1) * 512],
                                  start=k == 0, stop=k == KT - 1)
                last.then_inc(s["pe_o"], 1)

            project(0)
            for t in range(TT):
                if t + 1 < TT:
                    project(t + 1)
                r = rows_of(t)
                pe.wait_ge(s["h2_done"], t + 1)
                if t >= 2:
                    pe.wait_ge(s["h2T_ev"], t - 1)
                b = 4 + 2 * (t % 2)
                for k in range(KT):
                    last = pe.transpose(PS[:, b + k // 4, (k % 4) * r:(k % 4 + 1) * r],
                                        h2b[t % 2][0:r, k * 128:(k + 1) * 128], ident[0:r, 0:r])
                last.then_inc(s["pe_h2T"], 1)
            pe.wait_ge(s["keys_ld"], 16)
            for c in range(2 * PH):
                if c % 4 == 0:
                    pe.wait_ge(s["x1_done"], TT)
                last = pe.transpose(PS[:, c // 4, (c % 4) * 128:(c % 4 + 1) * 128], keysN[:, c, :], ident[:, :])
            last.then_inc(s["pe_k"], 1)
            pe.wait_ge(s["h2T_ev"], TT)
            pe.wait_ge(s["k_ev"], 1)

            def queries(c):
                pe.wait_ge(wq_ld[c % 8], 16 * (c // 8 + 1))
                if c >= 1:
                    pe.wait_ge(s["q_ev"], c)
                for j in range(3):
                    for k in range(KT):
                        last = mm(PS[:, j, 0:TH], wq[c % 8][:, k, :], h2T[:, k, j * TH:(j + 1) * TH], start=k == 0, stop=k == KT - 1)
                last.then_inc(s["pe_q"], 1)

            queries(0)
            for c in range(2 * PH):
                pe.wait_ge(s["q_ev"], c + 1)
                if c + 1 < 2 * PH:
                    queries(c + 1)
                b = 3 if c % 2 == 0 else 6
                if c >= 2:
                    pe.wait_ge(s["sc_ev"], c - 1)
                for t in range(PT):
                    last = mm(PS[:, b + t // 4, (t % 4) * 128:(t % 4 + 1) * 128], qTc[c % 2][:, t * 128:(t + 1) * 128], keysT[:, c, :],
                              start=True, stop=True)
                last.then_inc(s["pe_s"], 1)
            for c in range(2 * PH):
                h, half = c // 2, c % 2
                q, u = h // 2, h % 2
                last = mm(PS[q * 32:(q + 1) * 32, 5, (u * 2 + half) * 128:(u * 2 + half + 1) * 128], qS[:, c, :], keysT[:, c, :],
                          start=True, stop=True)
            last.then_inc(s["pe_ss"], 1)

            def weigh(m, first, second):
                par, mm_ = m
                for b in range(NB):
                    pe.wait_ge(s["diag_ready"], mm_ * NB + (b + 1))
                    pe.wait_ge(v_ld[b], mm_ * (16 * BATCH) + 16 * BATCH)
                    if b == 0 and not (first or second):
                        pe.wait_ge(s["y_added"], mm_ - 1)
                    for k in range(b * BATCH, (b + 1) * BATCH):
                        for half in range(2):
                            last = mm(PS[:, 2 * par + half, :], diag[par][:, k, :], Vr[:, k, half * 512:(half + 1) * 512],
                                      start=k == 0, stop=k == TOPK - 1)
                    last.then_inc(s["pv_done"], 1)

            pe.wait_ge(s["sc_ev"], 2 * PH)
            weigh((0, 0), True, False)
            weigh((1, 1), False, True)
            pe.wait_ge(s["y_sum"], 1)
            for half in range(2):
                last = mm(PS[0:NSAMP, 4 + half, :], sel[:, :], Y[:, half * 512:(half + 1) * 512], start=True, stop=True)
            last.then_inc(s["pe_sel"], 1)
            with pe.Fori(0, PT) as t:
                for u in range(PH):
                    weigh((u % 2, t * PH + (u + 2)), False, False)

        @block.scalar
        def _(ac):
            act_ = ac.activation

            def square_sum(junk, x, r, done):
                act_(junk[0:r, :], x, ACT.Square, accum_out=ss[0:r, 0:1])
                ac.drain()
                act_(ss[0:r, 1:2], ss[0:r, 0:1], ACT.Sqrt, scale=1.0 / D, bias=epsb[0:r, :]).then_inc(done, 1)

            ac.wait_ge(s["const_ld"], 16 * NCONST)
            ac.wait_ge(s["ticked"], 1)
            act_(cexp, crow, ACT.Exp, scale=-1.0).then_inc(s["cexp_done"], 1)
            for t in range(TT + 1):
                if t < TT:
                    r = rows_of(t)
                    if t >= 2:
                        ac.wait_ge(s["h_done"], t - 1)
                    ac.dma_start(xin[t % 2][0:r, :], x_rows(t)).then_inc(x_ld[t % 2], 16)
                if t >= 1:
                    r = rows_of(t - 1)
                    if t >= 2:
                        ac.wait_ge(s["h_done"], t - 1)
                    ac.wait_ge(x_ld[(t - 1) % 2], 16 * ((t - 1) // 2 + 1))
                    square_sum(sqj, xin[(t - 1) % 2][0:r, :], r, s["ss_done"])
                    ac.wait_ge(s["pe_hT"], t)
                    b = 3 + 2 * ((t - 1) % 2)
                    c0 = (t - 1) * 128
                    act_(hT[:, 0:4, c0:c0 + r], PS[:, b, 0:4 * r].rearrange("p (k r) -> p k r", k=4), ACT.Copy)
                    act_(hT[:, 4:8, c0:c0 + r], PS[:, b + 1, 0:4 * r].rearrange("p (k r) -> p k r", k=4), ACT.Copy).then_inc(s["hT_ev"], 1)
            ac.wait_ge(s["mod_st"], 32)
            for ct in range(14):
                ac.wait_ge(s["pe_p2"], ct + 1)
                dst = [qT[:, i, :] for i in range(4)] + [kT, vT] + [bT[:, i, :] for i in range(4)] + [cgT[:, i, :] for i in range(4)]
                for j in range(3):
                    last = act_(dst[ct][:, j * TH:(j + 1) * TH], PS[:, 3 * (ct % 2) + j, 0:TH], ACT.Copy)
                last.then_inc(s["p2_evA"], 1)

            def evac(n):
                ac.wait_ge(s["pe_pt"], n + 1)
                if n >= 2:
                    ac.wait_ge(s["pe_pv"], n - 1)
                for half in ((1,) if n < 2 else (0, 1)):
                    last = act_(PTb[n % 2][:, half, :], PS[:, 4 + half, :], ACT.Copy)
                last.then_inc(s["pt_ev"], 1)

            def z_out(blk):
                ac.wait_ge(s["pe_pv"], 2 * blk + 2)
                act_(zT[:, 0:4, blk * 128:(blk + 1) * 128], PS[:, 6 + blk % 2, :].rearrange("p (i t) -> p i t", i=4), ACT.Copy).then_inc(s["z_ev"], 1)

            for n in range(2 * PT):
                ac.wait_ge(s["m_done"], n + 1)
                lo = 128 if n < 2 else 0
                for i in range(GRP):
                    act_(S[n % 2][:, i, lo:256], S[n % 2][:, i, lo:256], ACT.Exp, bias=negm[:, n % 2, i:i + 1],
                         accum_out=rs[:, n % 2, i:i + 1])
                act_(esk[:, n % 2, :], esk[:, n % 2, :], ACT.Exp).then_inc(s["e_done"], 1)
                if n >= 1:
                    evac(n - 1)
                if n >= 2 and n % 2 == 0:
                    z_out(n // 2 - 1)
            evac(2 * PT - 1)
            z_out(PT - 1)
            for kv in range(NKV):
                ac.wait_ge(s["sm_done"], kv + 1)
                act_(SS, SS, ACT.Exp)
                act_(ses[:, :], ses[:, :], ACT.Exp).then_inc(s["se_done"], 1)
                ac.wait_ge(s["spt_ps"], kv + 1)
                if kv:
                    ac.wait_ge(s["spv_ps"], 1)
                act_(PTc, PS[:, 4, 0:NS * 16].rearrange("p (n c) -> p n c", n=NS), ACT.Copy)
                act_(PTn, PS[0:NSAMP, 5, 0:NS * 16].rearrange("p (n c) -> p n c", n=NS), ACT.Copy).then_inc(s["spt_ev"], 1)
            ac.wait_ge(s["spv_ps"], NKV)
            act_(zT[:, 0:4, SEQ:T].rearrange("p i (n t) -> p n i t", n=NS),
                 PS[:, 6, 0:NS * 16].rearrange("p (n i t) -> p n i t", n=NS, i=4), ACT.Copy).then_inc(s["z_ev"], 1)

            for t in range(TT):
                r = rows_of(t)
                ac.wait_ge(s["x1_done"], t + 1)
                if t:
                    ac.wait_ge(s["h2_done"], t)
                square_sum(sqj4, x1b[t % 2][0:r, :], r, s["ss4_done"])
                ac.wait_ge(s["pe_h2T"], t + 1)
                b = 4 + 2 * (t % 2)
                c0 = t * 128
                act_(h2T[:, 0:4, c0:c0 + r], PS[:, b, 0:4 * r].rearrange("p (k r) -> p k r", k=4), ACT.Copy)
                act_(h2T[:, 4:8, c0:c0 + r], PS[:, b + 1, 0:4 * r].rearrange("p (k r) -> p k r", k=4), ACT.Copy).then_inc(s["h2T_ev"], 1)
            for c in range(2 * PH):
                ac.wait_ge(s["pe_q"], c + 1)
                if c >= 2:
                    ac.wait_ge(s["pe_s"], c - 1)
                for j in range(3):
                    act_(qTc[c % 2][:, j * TH:(j + 1) * TH], PS[:, j, 0:TH], ACT.Copy)
                act_(qS[:, c, :], PS[:, 2, TH - NSAMP:TH], ACT.Copy).then_inc(s["q_ev"], 1)

            def weights(m, first, second):
                par, mm_ = m
                ac.wait_ge(s["idx_ready"], mm_ + 1)
                act_(gex[:, par, :], best[:, par, :], ACT.Exp, bias=nbest[:, par, :],
                     accum_out=gsum[:, par:par + 1]).then_inc(s["exp_done"], 1)
                ac.wait_ge(s["dots_done"], mm_ * NB + NB)
                act_(gel[:, par, :], act[:, par, :], ACT.Gelu).then_inc(s["gelu_done"], 1)
                ac.wait_ge(s["w_ready"], mm_ + 1)
                if not (first or second):
                    ac.wait_ge(s["pv_done"], mm_ * NB - NB)
                for k in range(TOPK):
                    last = act_(diag[par][:, k, :], ident[:, :], ACT.Copy, scale=wgt[:, par, k:k + 1])
                    if k % BATCH == BATCH - 1:
                        last.then_inc(s["diag_ready"], 1)

            ac.wait_ge(s["pe_ss"], 1)
            ac.wait_ge(s["scs_st"], 32)
            weights((0, 0), True, False)
            weights((1, 1), False, True)
            ac.wait_ge(s["y_sum"], 2)
            square_sum(sqj6, x2b[0:NSAMP, :], NSAMP, s["fin_ss"])
            with ac.Fori(0, PT) as t:
                for u in range(PH):
                    weights((u % 2, t * PH + (u + 2)), False, False)
                ac.wait_ge(s["y_sum"], t + 3)
                square_sum(sqj6, x2b, 128, s["fin_ss"])

        @block.vector
        def _(ve):
            def inv_rms(col, r):
                ms, root, y0, t, y1 = (rin[0:r, i:i + 1] for i in range(5))
                ve.tensor_scalar(ms, ss[0:r, 0:1], 1.0 / D, EPS, ALU.mult, ALU.add)
                ve.reciprocal(y0, ss[0:r, 1:2])
                ve.drain()
                ve.scalar_tensor_tensor(t, y0, y0, ms, ALU.mult, ALU.mult)
                ve.drain()
                ve.tensor_scalar(t, t, -0.5, 1.5, ALU.mult, ALU.add)
                ve.drain()
                ve.tensor_tensor(rinv[0:r, 1:2], y0, t, ALU.mult)
                ve.drain()

            ve.memset(tickv[:, :], 0.0)
            ve.memset(epsb[:, :], EPS)
            ve.drain().then_inc(s["ticked"], 1)
            ve.wait_ge(s["cexp_done"], 1)
            ve.tensor_scalar(cexp, cexp, 1.0, None, ALU.add)
            ve.drain()
            ve.reciprocal(cexp, cexp)
            ve.drain()
            ve.tensor_tensor(crow, crow, cexp, ALU.mult).then_inc(s["csil_done"], 1)
            ve.wait_ge(s["ct_ps"], 1)
            ve.tensor_copy(cw[:, :, :], PS[:, 0, 72:72 + 3 * CT].rearrange("p (j c) -> p j c", j=3))
            ve.tensor_copy(cT[:, :, :], PS[:, 0, 0:72].rearrange("p (k n) -> p k n", k=KT)).then_inc(s["ct_done"], 1)
            for g in range(12):
                c = slice(g * 512, (g + 1) * 512)
                ve.wait_ge(s["pe_mod"], g + 1)
                ve.tensor_tensor(modrow[:, c], PS[0:9, 1 + g % 2, :], brow[:, c], ALU.add).then_inc(s["mod_ev"], 1)
            ve.drain()
            ve.memset(uP[:, :, 0:2], 0.0)
            ve.wait_ge(s["vec1_ld"], 16 * (3 + 2 * TS))
            ve.scalar_tensor_tensor(A1, A1, 1.0, gmix, ALU.add, ALU.mult)
            ve.scalar_tensor_tensor(A1s, A1s, 1.0, gmix[0:NSAMP, :], ALU.add, ALU.mult)
            for t in range(TT):
                r = rows_of(t)
                x, h = xin[t % 2][0:r, :], hbuf[t % 2][0:r, :]
                A, B = (A1, B1) if t < PT else (A1s, B1s)
                ve.wait_ge(s["ss_done"], t + 1)
                inv_rms(0, r)
                if t >= 2:
                    ve.wait_ge(s["pe_hT"], t - 1)
                ve.scalar_tensor_tensor(h, x, rinv[0:r, 1:2], A, ALU.mult, ALU.mult)
                ve.drain()
                ve.tensor_tensor(h, h, B, ALU.add).then_inc(s["h_done"], 1)
            for c in range(CT):
                ct = 14 + c
                ve.wait_ge(s["p2_evA"], 14)
                ve.wait_ge(s["pe_p2"], ct + 1)
                for j in range(3):
                    b = 3 * (ct % 2) + j
                    w = min(TH, SEQ - j * TH)
                    last = ve.tensor_tensor(uP[:, c, 2 + j * TH:2 + j * TH + w], PS[:, b, 0:w], cgT[:, c, j * TH:j * TH + w], ALU.mult)
                    if w < TH:
                        last = ve.tensor_tensor(uS[:, c, :, 2:2 + TS], PS[:, b, w:TH].rearrange("p (n t) -> p n t", n=NS),
                                                cgT[:, c, SEQ:T].rearrange("p (n t) -> p n t", n=NS), ALU.mult)
                last.then_inc(s["p2_evD"], 1)
            ve.drain()
            for c in range(CT):
                ve.tensor_copy(utail[:, c, :].rearrange("p (n t) -> p n t", n=NS), uS[:, c, :, TS:TS + 2])
            for i in range(GRP):
                ve.tensor_copy(q16[:, :, i * TS:(i + 1) * TS], qT[:, i, SEQ:T].rearrange("p (n t) -> p n t", n=NS))
            for i in range(2):
                ve.wait_ge(s["pe_b"], i + 1)
                ve.tensor_copy(vnat[:, 4 * i:4 * i + 4, :], PS[:, 6 + i, :].rearrange("p (t c) -> p t c", t=4)).then_inc(s["b_ev"], 1)
            ve.wait_ge(s["pe_b"], 3)
            ve.tensor_copy(vnat[0:NSAMP, PT, :], PS[0:NSAMP, 0, 0:128])
            ve.tensor_copy(kn8, PS[0:NSAMP, 0, 128:256])
            ve.tensor_copy(kn7, PS[:, 0, 256:384]).then_inc(s["b_ev"], 1)
            ve.wait_ge(s["pe_b"], 4)
            for c in range(CT):
                last = ve.tensor_copy(uS[:, c, :, 0:2], PS[:, 1, c * 16:(c + 1) * 16].rearrange("p (n t) -> p n t", n=NS))
            last.then_inc(s["b_ev"], 1)
            for i in range(2):
                ve.wait_ge(s["pe_b"], 5 + i)
                ve.tensor_copy(cKT[:, 4 * i:4 * i + 4, :], PS[:, 4 + i, :].rearrange("p (t c) -> p t c", t=4)).then_inc(s["b_ev"], 1)
            ve.wait_ge(s["pe_b"], 7)
            ve.tensor_copy(utP, PS[0:2, 2, :]).then_inc(s["b_ev"], 1)
            ve.wait_ge(s["pe_b"], 8)
            ve.tensor_copy(utS, PS[0:16, 3, :]).then_inc(s["b_ev"], 1)

            ve.wait_ge(s["bias_ld"], 32)

            def soft1(n):
                par, kv, lo = n % 2, n % 2, 128 if n < 2 else 0
                ve.wait_ge(s["pe_sc"], n + 1)
                if n >= 2:
                    ve.wait_ge(s["pe_pt"], n - 1)
                ps = PS[:, 2 * par:2 * par + 2, :].rearrange("p b (i c) -> p (b i) c", i=2)
                ve.scalar_tensor_tensor(S[par][:, :, lo:256], ps[:, :, lo:256], DH ** -0.5,
                                        biasP[:, kv * GRP:(kv + 1) * GRP, lo:256], ALU.mult, ALU.add).then_inc(s["S_done"], 1)
                ve.drain()
                ve.tensor_reduce(mx[:, par, :], S[par][:, :, lo:256], AX.X, ALU.max)
                ve.drain()
                ve.tensor_tensor(mx[:, par, :], mx[:, par, :], sink[:, kv * GRP:(kv + 1) * GRP], ALU.max)
                ve.drain()
                ve.tensor_scalar(negm[:, par, :], mx[:, par, :], -1.0, None, ALU.mult)
                ve.tensor_tensor(esk[:, par, :], sink[:, kv * GRP:(kv + 1) * GRP], mx[:, par, :], ALU.subtract)
                ve.drain().then_inc(s["m_done"], 1)

            def soft2(n):
                par, lo = n % 2, 128 if n < 2 else 0
                ve.wait_ge(s["e_done"], n + 1)
                ve.tensor_tensor(rs[:, par, :], rs[:, par, :], esk[:, par, :], ALU.add)
                ve.drain()
                ve.reciprocal(rs[:, par, :], rs[:, par, :])
                ve.drain()
                ve.tensor_tensor(S[par][:, :, lo:256], S[par][:, :, lo:256],
                                 rs[:, par, :].unsqueeze(2).to_broadcast([128, GRP, 256 - lo]), ALU.mult).then_inc(s["p_done"], 1)

            soft1(0)
            for n in range(2 * PT):
                if n + 1 < 2 * PT:
                    soft1(n + 1)
                soft2(n)
            for kv in range(NKV):
                ve.wait_ge(s["pe_sc"], 2 * PT + kv + 1)
                ve.wait_ge(s["pe_pt"], 2 * PT)
                if kv:
                    ve.wait_ge(s["spt_ps"], 1)
                bs = biasS[:, kv, :].rearrange("p (n c) -> p n c", n=NS)
                ve.scalar_tensor_tensor(SS[:, :, 0:128], PS[0:16, 0:2, :].rearrange("p b (n c) -> p (b n) c", n=4), DH ** -0.5,
                                        bs[:, :, 0:128], ALU.mult, ALU.add)
                ve.scalar_tensor_tensor(SS[:, :, 128:160], PS[0:16, 2, 0:256].rearrange("p (n c) -> p n c", n=NS), DH ** -0.5,
                                        bs[:, :, 128:160], ALU.mult, ALU.add).then_inc(s["sss_done"], 1)
                ve.drain()
                ve.tensor_reduce(smx[:, :], SS, AX.X, ALU.max)
                ve.drain()
                ve.tensor_scalar(smx[:, :], smx[:, :], sinkS[:, kv:kv + 1], None, ALU.max)
                ve.drain()
                ve.tensor_tensor(SS, SS, smx[:, :].unsqueeze(2).to_broadcast([16, NS, 160]), ALU.subtract)
                ve.tensor_scalar(ses[:, :], smx[:, :], -1.0, sinkS[:, kv:kv + 1], ALU.mult, ALU.add)
                ve.drain().then_inc(s["sm_done"], 1)
                ve.wait_ge(s["se_done"], kv + 1)
                ve.tensor_reduce(sden[:, :], SS, AX.X, ALU.add)
                ve.drain()
                ve.tensor_tensor(sden[:, :], sden[:, :], ses[:, :], ALU.add)
                ve.drain()
                ve.reciprocal(sden[:, :], sden[:, :])
                ve.drain()
                ve.tensor_tensor(SS, SS, sden[:, :].unsqueeze(2).to_broadcast([16, NS, 160]), ALU.mult).then_inc(s["sp_done"], 1)

            for c in range(CT):
                zp, zs = zT[:, 4 + c, 0:SEQ], zT[:, 4 + c, SEQ:T].rearrange("p (n t) -> p n t", n=NS)
                ve.tensor_scalar(zp, uP[:, c, 0:SEQ], cw[:, 0, c:c + 1], None, ALU.mult)
                ve.tensor_scalar(zs, uS[:, c, :, 0:TS], cw[:, 0, c:c + 1], None, ALU.mult)
                for j in (1, 2):
                    ve.drain()
                    ve.scalar_tensor_tensor(zp, uP[:, c, j:j + SEQ], cw[:, j, c:c + 1], zp, ALU.mult, ALU.add)
                    ve.scalar_tensor_tensor(zs, uS[:, c, :, j:j + TS], cw[:, j, c:c + 1], zs, ALU.mult, ALU.add)
            ve.drain()
            ve.tensor_tensor(zT[:, 4:8, :], zT[:, 4:8, :], bT, ALU.mult).then_inc(s["z_conv"], 1)

            ve.wait_ge(s["vec4_ld"], 16 * (4 + 3 * TS))
            ve.wait_ge(s["g1_ld"], 16 * (6 + 2 * NS))
            ve.scalar_tensor_tensor(vec[1], vec[1], 1.0, gffn, ALU.add, ALU.mult)
            ve.scalar_tensor_tensor(vecs[1], vecs[1], 1.0, gffn[0:NSAMP, :], ALU.add, ALU.mult)
            for t in range(TT):
                r, i = rows_of(t), t % 2
                v = vec if t < PT else vecs
                x, x1, h2 = x4[i][0:r, :], x1b[i][0:r, :], h2b[i][0:r, :]
                ve.wait_ge(s["pe_o"], t + 1)
                if t >= 2:
                    ve.wait_ge(x1_st[i], 32 * (t // 2))
                    ve.wait_ge(s["pe_h2T"], t - 1)
                ve.tensor_tensor(x1, PS[0:r, 2 * i:2 * i + 2, :].rearrange("p b c -> p (b c)"), v[0][0:r, :], ALU.mult)
                ve.wait_ge(x4_ld[i], 16 * (t // 2 + 1))
                ve.drain()
                ve.tensor_tensor(x1, x1, x, ALU.add).then_inc(s["x1_done"], 1)
                ve.wait_ge(s["ss4_done"], t + 1)
                inv_rms(0, r)
                ve.scalar_tensor_tensor(h2, x1, rinv[0:r, 1:2], v[1][0:r, :], ALU.mult, ALU.mult)
                ve.drain()
                ve.tensor_tensor(h2, h2, v[2][0:r, :], ALU.add).then_inc(s["h2_done"], 1)
            ve.wait_ge(s["pe_k"], 1)
            ve.tensor_copy(keysT, PS[:, 0:4, :].rearrange("p b (k c) -> p (b k) c", k=4)).then_inc(s["k_ev"], 1)
            for c in range(2 * PH):
                h, half = c // 2, c % 2
                ve.wait_ge(s["pe_s"], c + 1)
                if h >= 2 and half == 0:
                    ve.wait_ge(sc_st[h % 2], 16 * (h // 2))
                b = 3 if half == 0 else 6
                ve.tensor_copy(scE[h % 2][:, :, half * 128:(half + 1) * 128],
                               PS[:, b:b + 2, :].rearrange("p b (t c) -> p (b t) c", t=4)).then_inc(s["sc_ev"], 1)
            ve.wait_ge(s["pe_ss"], 1)
            ve.tensor_copy(scS, PS[:, 5, :].rearrange("p (u c) -> p u c", u=2)).then_inc(s["scs_ev"], 1)
            for i in range(2):
                ve.wait_ge(sc_st[i], 64)
            ve.wait_ge(s["scs_st"], 32)

            def top(m, early):
                par, mm_, half_mm = m
                if not early:
                    ve.wait_ge(s["pv_done"], mm_ * NB - NB)
                ve.wait_ge(sc_ld[par], half_mm * 16 + 16)
                ve.memset(tickv[:, 0:1], 0.0)
                sc = scb[par]
                for p in range(2):
                    ve.max(topv[:, p, 0:8], sc[:, p, :])
                ve.drain()
                for p in range(2):
                    ve.max_index(topi[:, p, 0:8], topv[:, p, 0:8], sc[:, p, :])
                    ve.match_replace(sc2[:, p, :], topv[:, p, 0:8], sc[:, p, :], LOW)
                ve.drain()
                for p in range(2):
                    ve.max(topv[:, p, 8:16], sc2[:, p, :])
                ve.drain()
                for p in range(2):
                    ve.max_index(topi[:, p, 8:16], topv[:, p, 8:16], sc2[:, p, :])
                ve.tensor_tensor(cand, topv[:, 0, :].unsqueeze(2).to_broadcast([128, TOPK, TOPK]),
                                 topv[:, 1, :].unsqueeze(1).to_broadcast([128, TOPK, TOPK]), ALU.add)
                ve.drain()
                ve.tensor_copy(topf[:, :, :], topi[:, :, :])
                cf = cand.rearrange("p a b -> p (a b)")
                ve.max(best[:, par, 0:8], cf)
                ve.drain()
                ve.max_index(pos[:, 0:8], best[:, par, 0:8], cf)
                ve.match_replace(cand2, best[:, par, 0:8], cf, LOW)
                ve.tensor_scalar(nbest[:, par, :], best[:, par, 0:1], -1.0, None, ALU.mult)
                ve.drain()
                ve.max(best[:, par, 8:16], cand2)
                ve.drain()
                ve.max_index(pos[:, 8:16], best[:, par, 8:16], cand2)
                ve.drain()
                ve.tensor_scalar(posx[:, 0, :], pos[:, :], 4, None, ALU.logical_shift_right)
                ve.tensor_scalar(posx[:, 1, :], pos[:, :], 15, None, ALU.bitwise_and)
                ve.drain()
                ve.tensor_copy(posf[:, :, :], posx[:, :, :])
                ve.drain()
                for p, o in ((0, oh), (1, oh2)):
                    ve.tensor_tensor(o, iota[:, :].unsqueeze(1).to_broadcast([128, TOPK, TOPK]),
                                     posf[:, p, :].unsqueeze(2).to_broadcast([128, TOPK, TOPK]), ALU.is_equal)
                ve.drain()
                for p, o in ((0, oh), (1, oh2)):
                    ve.tensor_tensor(o, o, topf[:, p, :].unsqueeze(1).to_broadcast([128, TOPK, TOPK]), ALU.mult)
                ve.drain()
                for p, o in ((0, oh), (1, oh2)):
                    ve.tensor_reduce(ef[:, p, :], o, AX.X, ALU.add)
                ve.drain()
                ve.scalar_tensor_tensor(eid[par][:, :], ef[:, 0, :], float(NK), ef[:, 1, :], ALU.mult, ALU.add).then_inc(s["idx_ready"], 1)

            def dots(m):
                par, mm_ = m
                for b in range(NB):
                    ve.wait_ge(u_ld[b], mm_ * (16 * BATCH) + 16 * BATCH)
                    for k in range(b * BATCH, (b + 1) * BATCH):
                        last = ve.tensor_tensor_reduce(out=Ur[:, k, :], in0=Ur[:, k, :], in1=h2c, scale=1.0, scalar=0.0, op0=ALU.mult,
                                                       op1=ALU.add, accum_out=act[:, par, k:k + 1])
                    last.then_inc(s["dots_done"], 1)

            def weight(m):
                par, mm_ = m
                ve.wait_ge(s["exp_done"], mm_ + 1)
                ve.reciprocal(grec[:, par:par + 1], gsum[:, par:par + 1])
                ve.wait_ge(s["gelu_done"], mm_ + 1)
                ve.memset(tickv[:, 0:1], 0.0)
                ve.drain()
                ve.scalar_tensor_tensor(wgt[:, par, :], gex[:, par, :], grec[:, par:par + 1], gel[:, par, :],
                                        ALU.mult, ALU.mult).then_inc(s["w_ready"], 1)

            def gather_sum(m, first):
                par, mm_ = m
                ve.wait_ge(s["pv_done"], mm_ * NB + NB)
                ps = PS[:, 2 * par:2 * par + 2, :].rearrange("p b c -> p (b c)")
                if first:
                    ve.tensor_copy(Y, ps).then_inc(s["y_added"], 1)
                else:
                    ve.tensor_tensor(Y, Y, ps, ALU.add).then_inc(s["y_added"], 1)

            top((0, 0, 0), True)
            top((1, 1, 0), True)
            ve.wait_ge(s["h2s_ld"], 64)
            dots((0, 0))
            weight((0, 0))
            gather_sum((0, 0), True)
            top((0, 2, 1), False)
            dots((1, 1))
            weight((1, 1))
            ve.drain()
            gather_sum((1, 1), False)
            ve.drain().then_inc(s["y_sum"], 1)
            ve.wait_ge(s["pe_sel"], 1)
            ve.wait_ge(s["vec6_ld"], 16 * (2 + TS))
            ve.tensor_tensor(x2b[0:NSAMP, :], PS[0:NSAMP, 4:6, :].rearrange("p b c -> p (b c)"), g2s, ALU.mult)
            ve.wait_ge(s["x1_ld"], 16)
            ve.drain()
            ve.tensor_tensor(x2b[0:NSAMP, :], x2b[0:NSAMP, :], x1c[0:NSAMP, :], ALU.add).then_inc(s["y_sum"], 1)
            ve.wait_ge(s["fin_ss"], 1)
            inv_rms(0, NSAMP)
            ve.scalar_tensor_tensor(yb[0:NSAMP, :], x2b[0:NSAMP, :], rinv[0:NSAMP, 1:2], gfv[0:NSAMP, :], ALU.mult,
                                    ALU.mult).then_inc(s["y_out"], 1)
            with ve.Fori(0, PT) as t:
                for u in range(PH):
                    m = (u % 2, t * PH + (u + 2))
                    top(((u + 1) % 2, t * PH + (u + 3), t * (PH // 2) + (u + 3) // 2), False)
                    if u == 0:
                        ve.wait_ge(s["h2_ld"], t * 16 + 16)
                        ve.memset(tickv[:, 0:1], 0.0)
                    dots(m)
                    if u >= 1:
                        ve.drain()
                        gather_sum(((u - 1) % 2, t * PH + (u + 1)), u == 1)
                    weight(m)
                ve.drain()
                gather_sum(((PH - 1) % 2, t * PH + (PH + 1)), False)
                ve.drain()
                ve.tensor_tensor(x2b, Y, g2v, ALU.mult)
                ve.wait_ge(s["x1_ld"], t * 16 + 32)
                ve.memset(tickv[:, 0:1], 0.0)
                ve.drain()
                ve.tensor_tensor(x2b, x2b, x1c, ALU.add).then_inc(s["y_sum"], 1)
                ve.wait_ge(s["fin_ss"], t + 2)
                inv_rms(0, 128)
                ve.wait_ge(s["out_st"], t * 16 + 16)
                ve.scalar_tensor_tensor(yb, x2b, rinv[:, 1:2], gfv, ALU.mult, ALU.mult).then_inc(s["y_out"], 1)


def constants():
    slopes = [2.0 ** -(h + 1) for h in range(NH)]
    d = np.arange(128)[:, None] + 128 - np.arange(256)[None, :]
    ok = (d >= 0) & (d < WIN)
    alibi_p = np.stack([np.where(ok, -sl * d, NEG) for sl in slopes], 1).astype(np.float32)
    alibi_s = np.full((16, NKV, NS, 160), NEG, np.float32)
    for kv in range(NKV):
        for i in range(GRP):
            for t in range(TS):
                for n in range(NS):
                    sl, row = slopes[kv * GRP + i], i * TS + t
                    for key in range(128 + TS):
                        dist = 128 + t - key
                        if 0 <= dist < WIN:
                            alibi_s[row, kv, n, key if key < 128 else 128 + n * TS + key - 128] = -sl * dist
    return {"ident": np.eye(128, dtype=np.float32), "sel": np.tile(np.eye(NSAMP, dtype=np.float32), (4, 1)),
            "iota": np.tile(np.arange(TOPK, dtype=np.float32), (128, 1)), "alibi_p": alibi_p,
            "alibi_s": alibi_s.reshape(16, NKV, NS * 160)}


_SHAPES = {
    "x_prompt": (SEQ, D), "x_sample": (NSAMP, D), "c_prompt": (1, D), "c_sample": (NS, D), "cache_k": (NS, WIN, 128),
    "cache_v": (NS, WIN, 128), "state_conv": (2 * NS, DC), "norm_mix_g": (D,), "norm_ffn_g": (D,), "w_ada": (D, NADA * D),
    "b_ada": (NADA * D,), "w_in": (D, INC), "conv_w": (3, DC), "attn_sinks": (NH,), "w_out": (D, D),
    "peer_wq": (D, PH * 256), "peer_keys": (PH, 2, NK, 128), "peer_u": (NK * NK, D), "peer_v": (NK * NK, D),
    "norm_final_g": (D,),
}
_OUTS = {
    "y_prompt": ((SEQ, D), (1, SEQ, D)), "y_sample": ((NSAMP, D), (NS, TS, D)),
    "k_prompt": ((128, 128), (1, 1, WIN, NKV, DH)), "v_prompt": ((128, 128), (1, 1, WIN, NKV, DH)),
    "conv_prompt": ((2, DC), (1, 1, 2, DC)), "k_sample": ((NS, WIN, 128), (1, NS, WIN, NKV, DH)),
    "v_sample": ((NS, WIN, 128), (1, NS, WIN, NKV, DH)), "conv_sample": ((2 * NS, DC), (1, NS, 2, DC)),
}


def kernel(**inputs):
    import numpy as _np
    import concourse.bacc as _bacc
    from concourse import mybir as _mybir
    from concourse.bass_utils import run_bass_kernel_spmd as _run

    nc = _bacc.Bacc("TRN2", target_bir_lowering=False, num_devices=1)
    arrays = {f"in_{n}": _np.ascontiguousarray(inputs[n]).reshape(shape) for n, shape in _SHAPES.items()}
    arrays |= {f"in_{n}": v for n, v in constants().items()}
    a = {n[3:]: nc.dram_tensor(n, v.shape, _mybir.dt.from_np(v.dtype), kind="ExternalInput").ap() for n, v in arrays.items()}
    out = {n: nc.dram_tensor(f"out_{n}", shape, _mybir.dt.float32, kind="ExternalOutput").ap() for n, (shape, _) in _OUTS.items()}
    build(nc, a, out)
    r = _run(nc, [arrays], core_ids=[0])
    return tuple(r.results[0][f"out_{n}"].reshape(full) for n, (_, full) in _OUTS.items())
```

```python
from contextlib import ExitStack

import numpy as np

import concourse.bass as bass
from concourse import mybir

D = 1024
KT = D // 128
SEQ, NS, TS = 1024, 8, 4
NSAMP = NS * TS
T = SEQ + NSAMP
PT = SEQ // 128
TT = PT + 1
TH = T // 3
DH, NH, NKV = 64, 8, 2
GRP = NH // NKV
WIN = 128
DC = 512
CT = DC // 128
INC = 512 + 256 + 3 * DC
NADA = 6
PH, NK, TOPK = 8, 128, 16
CAND = TOPK * TOPK
UNITS = 2 + PT * PH
EPS = 1e-6
NEG = -1e30
LOW = -3.0e38
BATCH = 4
NB = TOPK // BATCH
RING = 2 * BATCH

f32 = mybir.dt.float32
i32 = mybir.dt.int32
u32 = mybir.dt.uint32
ALU = mybir.AluOpType
ACT = mybir.ActivationFunctionType
AX = mybir.AxisListType


def rows_of(t):
    return 128 if t < PT else NSAMP


def build(nc, a, out):
    ctx = ExitStack()
    with ctx:
        def sb(name, shape, dt=f32):
            return ctx.enter_context(nc.sbuf_tensor(name, shape, dt))

        def sem(name):
            return ctx.enter_context(nc.semaphore(name))

        mod_d = nc.dram_tensor("mod_d", (1 + NS, NADA * D), f32, kind="Internal").ap()
        x1_d = nc.dram_tensor("x1_d", (T, D), f32, kind="Internal").ap()
        h2_d = nc.dram_tensor("h2_d", (T, D), f32, kind="Internal").ap()
        h2T_d = nc.dram_tensor("h2T_d", (PT + 1, 128, D), f32, kind="Internal").ap()

        arena = sb("arena", [128, 51600])

        def R(off, *shape, p=128):
            n = int(np.prod(shape))
            v = arena[0:p, off:off + n]
            if len(shape) == 2:
                v = v.rearrange("p (a b) -> p a b", a=shape[0])
            if len(shape) == 3:
                v = v.rearrange("p (a b c) -> p a b c", a=shape[0], b=shape[1])
            return v

        hT = R(0, KT, T)
        crow, cexp = R(0, D, p=9), R(1024, D, p=9)
        wada = [R(8448, KT, 512), R(12544, KT, 512)]
        modrow = R(16896, NADA * D, p=9)
        brow = R(23232, NADA * D, p=9)
        zT = R(8448, KT, T)
        qT = R(16896, 4, T)
        kT, vT = R(21120, T), R(22176, T)
        bT = R(23232, CT, T)
        uP = R(27456, CT, SEQ + 2)
        uS = R(31560, CT, NS, TS + 2)
        cgT = R(31752, CT, T)
        vnat = R(35976, TT, 128)
        A1s, B1s = R(35976, D, p=NSAMP), R(37000, D, p=NSAMP)
        gmix = R(38024, D)
        cKn, cKT, cVn = R(37128, NS, 128), R(38152, NS, 128), R(39176, NS, 128)
        win = [R(40200 + 1024 * i, KT, 128) for i in range(4)]
        biasP = R(40200, NH, 256)
        biasS = R(42248, NKV, NS * 160, p=16)
        xin = [R(44808 + 1024 * i, D) for i in range(2)]
        hbuf = [R(46856 + 1024 * i, D) for i in range(2)]
        sqj = R(31752, D)
        S = [R(o, GRP, 256) for o in (44808, 45832, 50184)]
        PTb = [R(46856 + 1024 * i, 2, 512) for i in range(2)]
        SS = R(44808, NS, 160, p=16)
        PTc, PTn = R(46856, NS, 16), R(46984, NS, 16, p=NSAMP)
        A1, B1 = R(48904, D), R(49928, D)
        kn7, kn8 = R(48904, 128), R(49032, 128, p=NSAMP)
        utP, utS = R(49160, DC, p=2), R(49672, DC, p=16)
        stn = R(50952, DC, p=16)
        wout = R(0, KT, D)
        h2Tb = [R(42248 + 1024 * i, KT, 128) for i in range(2)]
        vec = [R(25344 + 1024 * i, D) for i in range(3)]
        vecs = [R(28416 + 1024 * i, D, p=NSAMP) for i in range(3)]
        x4 = [R(31752 + 1024 * i, D) for i in range(2)]
        x1b = [R(33800 + 1024 * i, D) for i in range(2)]
        h2b = [R(35848 + 1024 * i, D) for i in range(2)]
        sqj4 = R(45320, D)
        gffn = R(44296, D)
        keysN = R(40200, 2 * PH, 128)
        Ur = R(0, RING, D)
        Vr = R(8192, RING, D)
        wqh = [R(16896 + 8192 * i, KT, PH * 128) for i in range(2)]
        keysT, qTc = R(49280, 2 * PH, 128), R(51328, 2, 128)
        h2Tc = R(38400, KT, 128)
        scb = [R(47744 + 256 * i, 2, NK) for i in range(2)]
        h2c, x1c, Y, g2v, gfv = (R(33280 + 1024 * i, D) for i in range(5))
        diag = [R(39424 + 2048 * i, TOPK, 128) for i in range(2)]
        x2b, yb = R(43520, D), R(44544, D)
        g2s = R(45568, D, p=NSAMP)
        cand, cand2 = R(46592, TOPK, TOPK), R(46848, CAND)
        oh, oh2 = R(47104, TOPK, TOPK), R(47360, TOPK, TOPK)
        sc2 = R(47104, 2, NK)
        sqj6 = R(48256, D)

        h2TS, qS = sb("h2TS", [128, KT, NSAMP]), R(48256, 2 * PH, NSAMP)
        ident, sel = sb("ident", [128, 128]), sb("sel", [128, NSAMP])
        iota = sb("iota", [128, TOPK])
        sink = sb("sink", [128, NH])
        cw = sb("cw", [128, 3, CT])
        utail = sb("utail", [128, CT, 16])
        q16 = sb("q16", [128, NS, 16])
        cwn = sb("cwn", [3 * CT, 128])
        cT = sb("cT", [128, KT, 9])
        ss, rinv = sb("ss", [128, 2, 2]), sb("rinv", [128, 2])
        mx, negm, esk, rs = (sb(n, [128, 3, 4]) for n in ("mx", "negm", "esk", "rs"))
        smx, sden = sb("smx", [16, NS]), sb("sden", [16, NS])
        ses = sb("ses", [16, NS])
        topv = sb("topv", [128, 2, TOPK])
        topi = sb("topi", [128, 2, TOPK], u32)
        topf = sb("topf", [128, 2, TOPK])
        best = sb("best", [128, 2, TOPK])
        nbest = sb("nbest", [128, 2, 1])
        pos = sb("pos", [128, TOPK], u32)
        posx = sb("posx", [128, 2, TOPK], u32)
        posf = sb("posf", [128, 2, TOPK])
        ef = sb("ef", [128, 2, TOPK])
        eid = [sb(f"eid{i}", [128, TOPK], i32) for i in range(4)]
        gex, gsum = sb("gex", [128, 2, TOPK]), sb("gsum", [128, 2])
        grec = sb("grec", [128, 2])
        act = sb("act", [128, 2, TOPK])
        gel = sb("gel", [128, 2, TOPK])
        wgt = sb("wgt", [128, 2, TOPK])
        rin, epsb = sb("rin", [128, 5]), sb("epsb", [128, 1])
        tickv = sb("tickv", [128, 4])
        sinkS = sb("sinkS", [16, NKV])
        PS = ctx.enter_context(nc.psum_tensor("PS", [128, 8, 512], f32))

        names = """const_ld table_ld cexp_done csil_done ct_ps ct_done pe_mod mod_ev mod_st vec1_ld ss_done h_done
            pe_hT hT_ev pe_p2 p2_evA p2_evD state_ld cache_ld pe_b b_ev bias_ld pe_sc S_done m_done e_done
            p_done pe_pt pt_ev pe_pv z_ev z_conv sss_done sm_done se_done sp_done spt_ps spt_ev spv_ps
            wout_ld vec4_ld pe_o x1_done ss4_done h2_done pe_h2T h2T_ev keys_ld pe_k k_ev pe_ss h2_ld x1_ld
            vec6_ld idx_ready exp_done dots_done gelu_done w_ready diag_ready pv_done y_added y_sum fin_ss
            y_out pe_sel out_st g1_ld h2s_ld ticked pool_turn conv_step h2T_st h2T_ld pe_qn qn_ev pe_sn
            sn_ev qs_ps qs_ev""".split()
        s = {n: sem(n) for n in names}
        wada_ld = [sem(f"wada_ld{i}") for i in range(2)]
        x_ld = [sem(f"x_ld{i}") for i in range(2)]
        win_ld = [sem(f"win_ld{i}") for i in range(4)]
        x4_ld = [sem(f"x4_ld{i}") for i in range(2)]
        x1_st = [sem(f"x1_st{i}") for i in range(2)]
        wq_ld = [sem(f"wq_ld{i}") for i in range(4)]
        u_ld = [sem(f"u_ld{i}") for i in range(2)]
        v_ld = [sem(f"v_ld{i}") for i in range(2)]

        block = ctx.enter_context(nc.Block())
        NCONST, NTAB = 5, 11

        def x_rows(t):
            return a["x_prompt"][t * 128:(t + 1) * 128, :] if t < PT else a["x_sample"]

        def in_cols(ct):
            return [(ct * 64, 64), (256 + ct * 64, 64)] if ct < 4 else [(ct * 128, 128)]

        @block.sync
        def _(sp):
            for dst, src in ((crow[0:1, :], a["c_prompt"]), (crow[1:9, :], a["c_sample"]), (ident[:, :], a["ident"]),
                             (brow, a["b_ada"].partition_broadcast(9))):
                sp.dma_start(dst, src).then_inc(s["const_ld"], 16)
            sp.dma_start(cwn[:, :], a["conv_w"].rearrange("j (c p) -> (j c) p", p=128)).then_inc(s["const_ld"], 16)
            wv = a["w_ada"].rearrange("(k p) c -> p k c", p=128)
            for g in range(12):
                if g >= 2:
                    sp.wait_ge(s["pe_mod"], g - 1)
                sp.dma_start(wada[g % 2], wv[:, :, g * 512:(g + 1) * 512]).then_inc(wada_ld[g % 2], 16)
            wv2 = a["w_in"].rearrange("(k p) c -> p k c", p=128)
            for ct in range(18):
                if ct >= 4:
                    sp.wait_ge(s["pe_p2"], ct - 3)
                n = 0
                for c0, w in in_cols(ct):
                    sp.dma_start(win[ct % 4][:, :, n:n + w], wv2[:, :, c0:c0 + w]).then_inc(win_ld[ct % 4], 16)
                    n += w
            sp.wait_ge(s["pe_p2"], 18)
            sp.dma_start(biasP, a["alibi_p"]).then_inc(s["bias_ld"], 16)
            sp.dma_start(biasS, a["alibi_s"]).then_inc(s["bias_ld"], 16)
            for kv in range(NKV):
                sp.dma_start(wout[kv * 64:(kv + 1) * 64, 0:4, :],
                             a["w_out"][kv * 256:(kv + 1) * 256, :].rearrange("(i d) c -> d i c", d=64)).then_inc(s["wout_ld"], 16)
            sp.dma_start(wout[:, 4:8, :], a["w_out"][512:1024, :].rearrange("(k p) c -> p k c", p=128)).then_inc(s["wout_ld"], 16)
            wqv = a["peer_wq"].rearrange("(k p) c -> p k c", p=128)
            sp.wait_ge(s["z_conv"], 1)
            for t in range(TT + 1):
                if t < TT:
                    r = rows_of(t)
                    if t >= 2:
                        sp.wait_ge(s["x1_done"], t - 1)
                    sp.dma_start(x4[t % 2][0:r, :], x_rows(t)).then_inc(x4_ld[t % 2], 16)
                if t >= 1:
                    r = rows_of(t - 1)
                    sp.wait_ge(s["x1_done"], t)
                    sp.dma_start(x1_d[(t - 1) * 128:(t - 1) * 128 + r, :], x1b[(t - 1) % 2][0:r, :]).then_inc(x1_st[(t - 1) % 2], 16)
                    sp.wait_ge(s["h2_done"], t)
                    sp.dma_start(h2_d[(t - 1) * 128:(t - 1) * 128 + r, :], h2b[(t - 1) % 2][0:r, :]).then_inc(x1_st[(t - 1) % 2], 16)
                if t == 1:
                    sp.wait_ge(s["spv_ps"], NKV)
                    sp.dma_start(keysN, a["peer_keys"].rearrange("h q n c -> n (h q) c")).then_inc(s["keys_ld"], 16)
                    for j in range(2):
                        sp.dma_start(wqh[0][:, :, j * 512:(j + 1) * 512], wqv[:, :, j * 512:(j + 1) * 512]).then_inc(wq_ld[j], 16)
                if 2 <= t < TT:
                    j = t - 1
                    sp.wait_ge(s["h2T_ev"], j + 1)
                    sp.dma_start(h2T_d[j, :, :].rearrange("p (k c) -> p k c", k=KT), h2Tb[j % 2]).then_inc(s["h2T_st"], 16)
            sp.wait_ge(s["h2_done"], TT)
            for j in range(2, 4):
                sp.dma_start(wqh[1][:, :, j * 512 - D:(j + 1) * 512 - D], wqv[:, :, j * 512:(j + 1) * 512]).then_inc(wq_ld[j], 16)
            sp.dma_start(h2T_d[PT, :, :].rearrange("p (k c) -> p k c", k=KT), h2Tc).then_inc(s["h2T_st"], 16)
            sp.wait_ge(s["h2T_st"], 16 * PT)
            sp.wait_ge(s["h2T_ev"], TT)
            for i in range(2):
                sp.wait_ge(x1_st[i], 16 * (10 if i == 0 else 8))

            for qd in range(4):
                sp.dma_start(h2c[qd * 32:(qd + 1) * 32, :], h2_d[SEQ:T, :]).then_inc(s["h2s_ld"], 16)
            sp.dma_start(x1c[0:NSAMP, :], x1_d[SEQ:T, :]).then_inc(s["x1_ld"], 16)
            sp.dma_start(g2v, mod_d[0, 5 * D:6 * D].partition_broadcast(128)).then_inc(s["vec6_ld"], 16)
            sp.dma_start(gfv, a["norm_final_g"].partition_broadcast(128)).then_inc(s["vec6_ld"], 16)
            for j in range(TS):
                sp.dma_start(g2s[j:NSAMP:TS, :], mod_d[1:9, 5 * D:6 * D]).then_inc(s["vec6_ld"], 16)

            def tile_loads(t, done):
                sp.wait_ge(s["dots_done"], t * (PH * NB) + 2 * NB)
                sp.dma_start(h2c, h2_d[bass.ds(t * 128, 128), :]).then_inc(s["h2_ld"], 16)
                sp.wait_ge(s["y_out"], t + 1)
                sp.dma_start(*done).then_inc(s["out_st"], 16)
                sp.dma_start(x1c, x1_d[bass.ds(t * 128, 128), :]).then_inc(s["x1_ld"], 16)
                sp.wait_ge(s["pe_qn"], t * PH + PH)
                sp.dma_start(h2Tc, h2T_d[bass.ds(t + 1, 1), :, :].rearrange("u p (k c) -> (u p) k c", k=KT)).then_inc(s["h2T_ld"], 16)

            tile_loads(0, (out["y_sample"], yb[0:NSAMP, :]))
            with sp.Fori(1, PT) as t:
                tile_loads(t, (out["y_prompt"][bass.ds(t * 128 - 128, 128), :], yb))
            sp.wait_ge(s["y_out"], PT + 1)
            sp.dma_start(out["y_prompt"][SEQ - 128:SEQ, :], yb).then_inc(s["out_st"], 16)
            sp.wait_ge(s["out_st"], 16 * TT)
            sp.wait_ge(s["h2T_ld"], 16 * PT)
            sp.wait_ge(s["g1_ld"], 16 * (6 + 2 * NS))

        @block.gpsimd
        def _(po):
            for dst, src in ((sel[:, :], a["sel"]), (iota[:, :], a["iota"]), (sink[:, :], a["attn_sinks"].partition_broadcast(128))):
                po.dma_start(dst, src).then_inc(s["table_ld"], 16)
            for kv in range(NKV):
                for i in range(GRP):
                    h = kv * GRP + i
                    po.dma_start(sinkS[i * TS:(i + 1) * TS, kv:kv + 1],
                                 a["attn_sinks"][h:h + 1].partition_broadcast(TS)).then_inc(s["table_ld"], 16)
            po.dma_start(stn, a["state_conv"]).then_inc(s["state_ld"], 16)
            po.wait_ge(s["mod_ev"], 4)
            po.dma_start(mod_d[:, 0:2 * D], modrow[:, 0:2 * D]).then_inc(s["mod_st"], 16)
            po.dma_start(gmix, a["norm_mix_g"].partition_broadcast(128)).then_inc(s["vec1_ld"], 16)
            po.wait_ge(s["mod_st"], 16)
            for dst, dsts, part in ((B1, B1s, 0), (A1, A1s, 1)):
                po.dma_start(dst, mod_d[0, part * D:(part + 1) * D].partition_broadcast(128)).then_inc(s["vec1_ld"], 16)
                for j in range(TS):
                    po.dma_start(dsts[j:NSAMP:TS, :], mod_d[1:9, part * D:(part + 1) * D]).then_inc(s["vec1_ld"], 16)
            po.wait_ge(s["mod_ev"], 12)
            po.dma_start(mod_d[:, 2 * D:6 * D], modrow[:, 2 * D:6 * D]).then_inc(s["mod_st"], 16)
            po.wait_ge(s["h_done"], TT)
            po.dma_start(cKn, a["cache_k"].rearrange("n s c -> s n c")).then_inc(s["cache_ld"], 16)
            po.dma_start(cVn, a["cache_v"].rearrange("n s c -> s n c")).then_inc(s["cache_ld"], 16)
            for name, src in (("k_sample", "cache_k"), ("v_sample", "cache_v")):
                po.dma_start(out[name][:, 0:WIN - TS, :], a[src][:, TS:WIN, :]).then_inc(s["g1_ld"], 16)
            po.wait_ge(s["b_ev"], 8)
            po.dma_start(out["k_prompt"], kn7).then_inc(s["g1_ld"], 16)
            po.dma_start(out["v_prompt"], vnat[:, PT - 1, :]).then_inc(s["g1_ld"], 16)
            po.dma_start(out["conv_prompt"], utP).then_inc(s["g1_ld"], 16)
            po.dma_start(out["conv_sample"], utS).then_inc(s["g1_ld"], 16)
            for n in range(NS):
                po.dma_start(out["k_sample"][n, WIN - TS:WIN, :], kn8[n * TS:(n + 1) * TS, :]).then_inc(s["g1_ld"], 16)
                po.dma_start(out["v_sample"][n, WIN - TS:WIN, :], vnat[n * TS:(n + 1) * TS, PT, :]).then_inc(s["g1_ld"], 16)
            seq = 0

            def step(*args, tt=False):
                nonlocal seq
                (po.tensor_tensor if tt else po.tensor_scalar)(*args).then_inc(s["conv_step"], 1)
                seq += 1
                return seq

            for c in range(CT):
                zp, zs = zT[:, 4 + c, 0:SEQ], zT[:, 4 + c, SEQ:T].rearrange("p (n t) -> p n t", n=NS)
                tp = [cgT[:, j, 0:SEQ] for j in (0, 1)]
                tn = [cgT[:, j, SEQ:T].rearrange("p (n t) -> p n t", n=NS) for j in (0, 1)]
                for z, t1, t2, src in ((zp, tp[0], tp[1], lambda j: uP[:, c, j:j + SEQ]),
                                       (zs, tn[0], tn[1], lambda j: uS[:, c, :, j:j + TS])):
                    step(z, src(0), cw[:, 0, c:c + 1], None, ALU.mult)
                    step(t1, src(1), cw[:, 1, c:c + 1], None, ALU.mult)
                    step(t2, src(2), cw[:, 2, c:c + 1], None, ALU.mult)
                    po.wait_ge(s["conv_step"], seq)
                    po.wait_ge(s["conv_step"], step(z, z, t1, ALU.add, tt=True))
                    po.wait_ge(s["conv_step"], step(z, z, t2, ALU.add, tt=True))
                step(zT[:, 4 + c, :], zT[:, 4 + c, :], bT[:, c, :], ALU.mult, tt=True)
                po.wait_ge(s["conv_step"], seq)
            po.sem_inc(s["z_conv"], 1)
            po.wait_ge(s["mod_st"], 32)
            for i, part in enumerate((2, 4, 3)):
                po.dma_start(vec[i], mod_d[0, part * D:(part + 1) * D].partition_broadcast(128)).then_inc(s["vec4_ld"], 16)
                for j in range(TS):
                    po.dma_start(vecs[i][j:NSAMP:TS, :], mod_d[1:9, part * D:(part + 1) * D]).then_inc(s["vec4_ld"], 16)
            po.wait_ge(s["pe_pv"], 16)
            po.wait_ge(s["spv_ps"], NKV)
            po.dma_start(gffn, a["norm_ffn_g"].partition_broadcast(128)).then_inc(s["vec4_ld"], 16)
            po.wait_ge(s["pe_o"], TT)
            for i in range(2):
                po.wait_ge(x1_st[i], 16 * (10 if i == 0 else 8))

            def gather(table, idx, m, b):
                ring, landed, used = (Ur, u_ld, "dots_done") if table == "peer_u" else (Vr, v_ld, "pv_done")
                if table == "peer_u" and b == 0:
                    po.wait_ge(s["idx_ready"], m + 1)
                if not isinstance(m, int) or m * NB + b >= 2:
                    po.wait_ge(s[used], m * NB + (b - 1))
                if not isinstance(m, int):
                    po.sem_inc(s["pool_turn"], 1)
                for k in range(BATCH):
                    po.indirect_dma_start(
                        out=ring[:, (b % 2) * BATCH + k, :], out_offset=None, in_=a[table],
                        in_offset=bass.IndirectOffsetOnAxis(ap=eid[idx][:, b * BATCH + k:b * BATCH + k + 1], axis=0),
                    ).then_inc(landed[b % 2], 16)

            def gathers(count, i0, m0):
                for u in range(count):
                    for b in range(NB):
                        gather("peer_u", (i0 + u) % 4, m0 + u, b)
                        if i0 + u:
                            gather("peer_v", (i0 + u - 1) % 4, m0 + (u - 1), b)

            gathers(2, 0, 0)
            gathers(PH, 2, 2)
            with po.Fori(1, PT) as t:
                gathers(PH, 2, t * PH + 2)
            for b in range(NB):
                gather("peer_v", (UNITS - 1) % 4, UNITS - 1, b)

        @block.tensor
        def _(pe):
            mm = pe.matmul
            pe.wait_ge(s["const_ld"], 16 * NCONST)
            pe.wait_ge(s["csil_done"], 1)
            for k in range(KT):
                last = pe.transpose(PS[:, 0, k * 9:(k + 1) * 9], crow[:, k * 128:(k + 1) * 128], ident[0:9, 0:9])
            last = pe.transpose(PS[:, 0, 72:72 + 3 * CT], cwn[:, :], ident[0:3 * CT, 0:3 * CT])
            last.then_inc(s["ct_ps"], 1)
            pe.wait_ge(s["ct_done"], 1)
            def modulate(g):
                pe.wait_ge(wada_ld[g % 2], 16 * (g // 2 + 1))
                if g >= 2:
                    pe.wait_ge(s["mod_ev"], g - 1)
                for k in range(KT):
                    last = mm(PS[0:9, 1 + g % 2, :], cT[:, k, :], wada[g % 2][:, k, :], start=k == 0, stop=k == KT - 1)
                last.then_inc(s["pe_mod"], 1)

            for g in range(6):
                modulate(g)
            for t in range(TT):
                r = rows_of(t)
                pe.wait_ge(s["h_done"], t + 1)
                if t >= 2:
                    pe.wait_ge(s["hT_ev"], t - 1)
                b = 3 + 2 * (t % 2)
                for k in range(KT):
                    last = pe.transpose(PS[:, b + k // 4, (k % 4) * r:(k % 4 + 1) * r],
                                        hbuf[t % 2][0:r, k * 128:(k + 1) * 128], ident[0:r, 0:r])
                last.then_inc(s["pe_hT"], 1)
                if t < 6:
                    modulate(6 + t)
            pe.wait_ge(s["hT_ev"], TT)
            for ct in range(18):
                pe.wait_ge(win_ld[ct % 4], 16 * sum(len(in_cols(c)) for c in range(ct % 4, ct + 1, 4)))
                if ct >= 2:
                    if ct - 2 < 14:
                        pe.wait_ge(s["p2_evA"], ct - 1)
                    else:
                        pe.wait_ge(s["p2_evD"], ct - 15)
                for j in range(3):
                    for k in range(KT):
                        last = mm(PS[:, 3 * (ct % 2) + j, 0:TH], win[ct % 4][:, k, :], hT[:, k, j * TH:(j + 1) * TH],
                                  start=k == 0, stop=k == KT - 1)
                last.then_inc(s["pe_p2"], 1)
            for t in range(PT):
                last = pe.transpose(PS[:, 6 + t // 4, (t % 4) * 128:(t % 4 + 1) * 128], vT[:, t * 128:(t + 1) * 128], ident[:, :])
                if t % 4 == 3:
                    last.then_inc(s["pe_b"], 1)
            pe.wait_ge(s["p2_evD"], 4)
            pe.transpose(PS[0:NSAMP, 0, 0:128], vT[:, SEQ:T], ident[:, :])
            pe.transpose(PS[0:NSAMP, 0, 128:256], kT[:, SEQ:T], ident[:, :])
            pe.transpose(PS[:, 0, 256:384], kT[:, SEQ - 128:SEQ], ident[:, :]).then_inc(s["pe_b"], 1)
            pe.wait_ge(s["state_ld"], 16)
            for c in range(CT):
                last = pe.transpose(PS[:, 1, c * 16:(c + 1) * 16], stn[:, c * 128:(c + 1) * 128], ident[0:16, 0:16])
            last.then_inc(s["pe_b"], 1)
            pe.wait_ge(s["cache_ld"], 32)
            for n in range(NS):
                last = pe.transpose(PS[:, 4 + n // 4, (n % 4) * 128:(n % 4 + 1) * 128], cKn[:, n, :], ident[:, :])
                if n % 4 == 3:
                    last.then_inc(s["pe_b"], 1)
            pe.wait_ge(s["b_ev"], 1)
            for c in range(CT):
                last = pe.transpose(PS[0:2, 2, c * 128:(c + 1) * 128], uP[:, c, SEQ:SEQ + 2], ident[:, :])
            last.then_inc(s["pe_b"], 1)
            for c in range(CT):
                last = pe.transpose(PS[0:16, 3, c * 128:(c + 1) * 128], utail[:, c, :], ident[:, :])
            last.then_inc(s["pe_b"], 1)
            pe.wait_ge(s["b_ev"], 8)

            def scores(n):
                blk, kv = n // 2, n % 2
                p, lo = kv * 64, 128 if blk == 0 else 0
                if n >= 2:
                    pe.wait_ge(s["S_done"], n - 1)
                for i in range(GRP):
                    last = mm(PS[:, 2 * (n % 2) + i // 2, (i % 2) * 256 + lo:(i % 2 + 1) * 256],
                              qT[p:p + 64, i, blk * 128:(blk + 1) * 128],
                              kT[p:p + 64, (blk - 1) * 128 + lo:(blk + 1) * 128], start=True, stop=True)
                last.then_inc(s["pe_sc"], 1)

            def values(n):
                blk, kv = n // 2, n % 2
                p = kv * 64
                pe.wait_ge(s["pt_ev"], n + 1)
                if kv == 0 and blk >= 2:
                    pe.wait_ge(s["z_ev"], blk - 1)
                for half in ((1,) if blk == 0 else (0, 1)):
                    last = mm(PS[p:p + 64, 6 + blk % 2, :], vnat[:, blk - 1 + half, p:p + 64], PTb[n % 2][:, half, :],
                              start=half == (1 if blk == 0 else 0), stop=half == 1)
                last.then_inc(s["pe_pv"], 1)

            scores(0)
            scores(1)
            for n in range(2 * PT):
                if n + 2 < 2 * PT:
                    scores(n + 2)
                pe.wait_ge(s["p_done"], n + 1)
                if n >= 1:
                    pe.wait_ge(s["pt_ev"], n)
                for half in ((1,) if n < 2 else (0, 1)):
                    for i in range(GRP):
                        last = pe.transpose(PS[:, 4 + half, i * 128:(i + 1) * 128], S[n % 3][:, i, half * 128:(half + 1) * 128], ident[:, :])
                last.then_inc(s["pe_pt"], 1)
                if n >= 1:
                    values(n - 1)
            values(2 * PT - 1)
            pe.wait_ge(s["S_done"], 2 * PT)
            for kv in range(NKV):
                p = kv * 64
                if kv:
                    pe.wait_ge(s["sss_done"], 1)
                for n in range(NS):
                    q = q16[p:p + 64, n, :]
                    mm(PS[0:16, n // 4, (n % 4) * 128:(n % 4 + 1) * 128], q, cKT[p:p + 64, n, :], start=True, stop=True)
                    last = mm(PS[0:16, 2, n * 32:(n + 1) * 32], q, kT[p:p + 64, SEQ:T], start=True, stop=True)
                last.then_inc(s["pe_sc"], 1)
                pe.wait_ge(s["sp_done"], kv + 1)
                pe.wait_ge(s["pt_ev"], 2 * PT)
                if kv:
                    pe.wait_ge(s["spt_ev"], 1)
                for n in range(NS):
                    pe.transpose(PS[:, 4, n * 16:(n + 1) * 16], SS[:, n, 0:128], ident[0:16, 0:16])
                    last = pe.transpose(PS[0:NSAMP, 5, n * 16:(n + 1) * 16], SS[:, n, 128:160], ident[0:16, 0:16])
                last.then_inc(s["spt_ps"], 1)
                pe.wait_ge(s["spt_ev"], kv + 1)
                if kv == 0:
                    pe.wait_ge(s["z_ev"], PT - 1)
                for n in range(NS):
                    mm(PS[p:p + 64, 6, n * 16:(n + 1) * 16], cVn[:, n, p:p + 64], PTc[:, n, :], start=True, stop=False)
                    last = mm(PS[p:p + 64, 6, n * 16:(n + 1) * 16], vnat[0:NSAMP, PT, p:p + 64], PTn[:, n, :], start=False, stop=True)
                last.then_inc(s["spv_ps"], 1)

            pe.wait_ge(s["wout_ld"], 48)
            pe.wait_ge(s["z_ev"], PT + 1)
            pe.wait_ge(s["z_conv"], 1)

            def project(t):
                r = rows_of(t)
                if t >= 2:
                    pe.wait_ge(s["x1_done"], t - 1)
                for half in range(2):
                    for k in range(KT):
                        last = mm(PS[0:r, 2 * (t % 2) + half, :], zT[:, k, t * 128:t * 128 + r], wout[:, k, half * 512:(half + 1) * 512],
                                  start=k == 0, stop=k == KT - 1)
                last.then_inc(s["pe_o"], 1)

            project(0)
            for t in range(TT):
                if t + 1 < TT:
                    project(t + 1)
                r = rows_of(t)
                pe.wait_ge(s["h2_done"], t + 1)
                if t >= 2:
                    pe.wait_ge(s["h2T_ev"], t - 1)
                b = 4 + 2 * (t % 2)
                for k in range(KT):
                    last = pe.transpose(PS[:, b + k // 4, (k % 4) * r:(k % 4 + 1) * r],
                                        h2b[t % 2][0:r, k * 128:(k + 1) * 128], ident[0:r, 0:r])
                last.then_inc(s["pe_h2T"], 1)
            pe.wait_ge(s["keys_ld"], 16)
            for c in range(2 * PH):
                if c % 4 == 0:
                    pe.wait_ge(s["x1_done"], TT)
                last = pe.transpose(PS[:, c // 4, (c % 4) * 128:(c % 4 + 1) * 128], keysN[:, c, :], ident[:, :])
            last.then_inc(s["pe_k"], 1)
            pe.wait_ge(s["h2T_ev"], TT)
            pe.wait_ge(s["k_ev"], 1)
            for c in range(2 * PH):
                if c % 4 == 0:
                    pe.wait_ge(wq_ld[c // 4], 16)
                for k in range(KT):
                    last = mm(PS[:, 4, c * NSAMP:(c + 1) * NSAMP], wqh[c // PH][:, k, (c % PH) * 128:(c % PH + 1) * 128], h2TS[:, k, :], start=k == 0, stop=k == KT - 1)
            last.then_inc(s["qs_ps"], 1)
            pe.wait_ge(s["qs_ev"], 1)
            for c in range(2 * PH):
                h, half = c // 2, c % 2
                q, u = h // 2, h % 2
                last = mm(PS[q * 32:(q + 1) * 32, 5, (u * 2 + half) * 128:(u * 2 + half + 1) * 128], qS[:, c, :], keysT[:, c, :],
                          start=True, stop=True)
            last.then_inc(s["pe_ss"], 1)

            def next_queries(h, m):
                if not isinstance(m, int) or m:
                    pe.wait_ge(s["qn_ev"], m)
                for half in range(2):
                    c = 2 * h + half
                    for k in range(KT):
                        last = mm(PS[:, 6, half * 128:(half + 1) * 128], wqh[c // PH][:, k, (c % PH) * 128:(c % PH + 1) * 128], h2Tc[:, k, :], start=k == 0, stop=k == KT - 1)
                last.then_inc(s["pe_qn"], 1)

            def next_scores(h, m):
                pe.wait_ge(s["qn_ev"], m + 1)
                if not isinstance(m, int) or m:
                    pe.wait_ge(s["sn_ev"], m)
                for half in range(2):
                    last = mm(PS[:, 7, half * 128:(half + 1) * 128], qTc[:, half, :], keysT[:, 2 * h + half, :], start=True, stop=True)
                last.then_inc(s["pe_sn"], 1)

            def weigh(par, m, b):
                pe.wait_ge(s["diag_ready"], m * NB + (b + 1))
                pe.wait_ge(v_ld[b % 2], m * (32 * BATCH) + 16 * BATCH * (b // 2 + 1))
                if b == 0 and (not isinstance(m, int) or m >= 2):
                    pe.wait_ge(s["y_added"], m - 1)
                for k in range(b * BATCH, (b + 1) * BATCH):
                    for half in range(2):
                        last = mm(PS[:, 2 * par + half, :], diag[par][:, k, :], Vr[:, k % RING, half * 512:(half + 1) * 512],
                                  start=k == 0, stop=k == TOPK - 1)
                last.then_inc(s["pv_done"], 1)

            def units(count, m0, t):
                for u in range(count):
                    h = (u + 2) % PH if count == PH else u
                    if count == PH and u == 1 and isinstance(t, int):
                        select()
                    if count == PH and u == PH - 2:
                        pe.wait_ge(s["h2T_ld"], t * 16 + 16)
                    next_queries(h, m0 + u)
                    for b in range(NB):
                        if count == PH or u:
                            weigh((u - 1) % 2, m0 + (u - 1), b)
                        if b == 0:
                            next_scores(h, m0 + u)

            def select():
                pe.wait_ge(s["y_sum"], 1)
                pe.wait_ge(s["table_ld"], 16 * NTAB)
                for half in range(2):
                    last = mm(PS[0:NSAMP, 4 + half, :], sel[:, :], Y[:, half * 512:(half + 1) * 512], start=True, stop=True)
                last.then_inc(s["pe_sel"], 1)

            pe.wait_ge(s["x1_done"], TT)
            units(2, 0, 0)
            units(PH, 2, 0)
            with pe.Fori(1, PT) as t:
                units(PH, t * PH + 2, t)
            for b in range(NB):
                weigh((UNITS - 1) % 2, UNITS - 1, b)

        @block.scalar
        def _(ac):
            act_ = ac.activation

            def square_sum(junk, x, r, par, done):
                act_(junk[0:r, :], x, ACT.Square, accum_out=ss[0:r, par, 0:1])
                ac.drain()
                act_(ss[0:r, par, 1:2], ss[0:r, par, 0:1], ACT.Sqrt, scale=1.0 / D, bias=epsb[0:r, :]).then_inc(done, 1)

            ac.wait_ge(s["const_ld"], 16 * NCONST)
            ac.wait_ge(s["ticked"], 1)
            act_(cexp, crow, ACT.Exp, scale=-1.0).then_inc(s["cexp_done"], 1)
            def load_x(t):
                if t >= 2:
                    ac.wait_ge(s["h_done"], t - 1)
                ac.dma_start(xin[t % 2][0:rows_of(t), :], x_rows(t)).then_inc(x_ld[t % 2], 16)

            load_x(0)
            load_x(1)
            for t in range(TT + 1):
                if t < TT:
                    ac.wait_ge(x_ld[t % 2], 16 * (t // 2 + 1))
                    square_sum(sqj, xin[t % 2][0:rows_of(t), :], rows_of(t), t % 2, s["ss_done"])
                if t >= 1:
                    r, c0, b = rows_of(t - 1), (t - 1) * 128, 3 + 2 * ((t - 1) % 2)
                    ac.wait_ge(s["pe_hT"], t)
                    act_(hT[:, 0:4, c0:c0 + r], PS[:, b, 0:4 * r].rearrange("p (k r) -> p k r", k=4), ACT.Copy)
                    act_(hT[:, 4:8, c0:c0 + r], PS[:, b + 1, 0:4 * r].rearrange("p (k r) -> p k r", k=4), ACT.Copy).then_inc(s["hT_ev"], 1)
                    if t + 1 < TT:
                        load_x(t + 1)
            ac.wait_ge(s["mod_st"], 32)
            for ct in range(14):
                ac.wait_ge(s["pe_p2"], ct + 1)
                dst = [qT[:, i, :] for i in range(4)] + [kT, vT] + [bT[:, i, :] for i in range(4)] + [cgT[:, i, :] for i in range(4)]
                for j in range(3):
                    last = act_(dst[ct][:, j * TH:(j + 1) * TH], PS[:, 3 * (ct % 2) + j, 0:TH], ACT.Copy)
                last.then_inc(s["p2_evA"], 1)

            def evac(n):
                ac.wait_ge(s["pe_pt"], n + 1)
                if n >= 2:
                    ac.wait_ge(s["pe_pv"], n - 1)
                for half in ((1,) if n < 2 else (0, 1)):
                    last = act_(PTb[n % 2][:, half, :], PS[:, 4 + half, :], ACT.Copy)
                last.then_inc(s["pt_ev"], 1)

            def z_out(blk):
                ac.wait_ge(s["pe_pv"], 2 * blk + 2)
                act_(zT[:, 0:4, blk * 128:(blk + 1) * 128], PS[:, 6 + blk % 2, :].rearrange("p (i t) -> p i t", i=4), ACT.Copy).then_inc(s["z_ev"], 1)

            for n in range(2 * PT):
                ac.wait_ge(s["m_done"], n + 1)
                lo = 128 if n < 2 else 0
                for i in range(GRP):
                    act_(S[n % 3][:, i, lo:256], S[n % 3][:, i, lo:256], ACT.Exp, bias=negm[:, n % 3, i:i + 1],
                         accum_out=rs[:, n % 3, i:i + 1])
                act_(esk[:, n % 3, :], esk[:, n % 3, :], ACT.Exp).then_inc(s["e_done"], 1)
                if n >= 1:
                    evac(n - 1)
                if n >= 2 and n % 2 == 0:
                    z_out(n // 2 - 1)
            evac(2 * PT - 1)
            z_out(PT - 1)
            for kv in range(NKV):
                ac.wait_ge(s["sm_done"], kv + 1)
                act_(SS, SS, ACT.Exp)
                act_(ses[:, :], ses[:, :], ACT.Exp).then_inc(s["se_done"], 1)
                ac.wait_ge(s["spt_ps"], kv + 1)
                if kv:
                    ac.wait_ge(s["spv_ps"], 1)
                act_(PTc, PS[:, 4, 0:NS * 16].rearrange("p (n c) -> p n c", n=NS), ACT.Copy)
                act_(PTn, PS[0:NSAMP, 5, 0:NS * 16].rearrange("p (n c) -> p n c", n=NS), ACT.Copy).then_inc(s["spt_ev"], 1)
            ac.wait_ge(s["spv_ps"], NKV)
            act_(zT[:, 0:4, SEQ:T].rearrange("p i (n t) -> p n i t", n=NS),
                 PS[:, 6, 0:NS * 16].rearrange("p (n i t) -> p n i t", n=NS, i=4), ACT.Copy).then_inc(s["z_ev"], 1)

            for t in range(TT + 1):
                if t < TT:
                    r = rows_of(t)
                    ac.wait_ge(s["x1_done"], t + 1)
                    if t >= 2:
                        ac.wait_ge(s["h2_done"], t - 1)
                    square_sum(sqj4, x1b[t % 2][0:r, :], r, t % 2, s["ss4_done"])
                if t == 0:
                    continue
                r, b = rows_of(t - 1), 4 + 2 * ((t - 1) % 2)
                ac.wait_ge(s["pe_h2T"], t)
                dst = h2Tc if t == 1 else h2Tb[(t - 1) % 2] if t <= PT else h2TS
                if 4 <= t <= PT:
                    ac.wait_ge(s["h2T_st"], 16 * (t - 3))
                act_(dst[:, 0:4, :], PS[:, b, 0:4 * r].rearrange("p (k r) -> p k r", k=4), ACT.Copy)
                act_(dst[:, 4:8, :], PS[:, b + 1, 0:4 * r].rearrange("p (k r) -> p k r", k=4), ACT.Copy)
                ac.drain().then_inc(s["h2T_ev"], 1)
            ac.wait_ge(s["qs_ps"], 1)
            act_(qS, PS[:, 4, :].rearrange("p (c t) -> p c t", c=2 * PH), ACT.Copy).then_inc(s["qs_ev"], 1)

            def weights(m):
                par, mm_ = m
                ac.wait_ge(s["idx_ready"], mm_ + 1)
                act_(gex[:, par, :], best[:, par, :], ACT.Exp, bias=nbest[:, par, :],
                     accum_out=gsum[:, par:par + 1]).then_inc(s["exp_done"], 1)
                ac.wait_ge(s["pe_qn"], mm_ + 1)
                if not isinstance(mm_, int) or mm_:
                    ac.wait_ge(s["pe_sn"], mm_)
                act_(qTc, PS[:, 6, 0:256].rearrange("p (a b) -> p a b", a=2), ACT.Copy).then_inc(s["qn_ev"], 1)
                ac.wait_ge(s["pe_sn"], mm_ + 1)
                act_(scb[par], PS[:, 7, 0:256].rearrange("p (a b) -> p a b", a=2), ACT.Copy).then_inc(s["sn_ev"], 1)
                ac.wait_ge(s["dots_done"], mm_ * NB + NB)
                act_(gel[:, par, :], act[:, par, :], ACT.Gelu).then_inc(s["gelu_done"], 1)
                ac.wait_ge(s["w_ready"], mm_ + 1)
                if not isinstance(mm_, int) or mm_ >= 2:
                    ac.wait_ge(s["pv_done"], mm_ * NB - NB)
                for k in range(TOPK):
                    last = act_(diag[par][:, k, :], ident[:, :], ACT.Copy, scale=wgt[:, par, k:k + 1])
                    if k % BATCH == BATCH - 1:
                        last.then_inc(s["diag_ready"], 1)

            ac.wait_ge(s["pe_ss"], 1)
            weights((0, 0))
            weights((1, 1))
            weights((0, 2))
            ac.wait_ge(s["y_sum"], 2)
            square_sum(sqj6, x2b[0:NSAMP, :], NSAMP, 0, s["fin_ss"])
            for u in range(1, PH):
                weights((u % 2, u + 2))
            with ac.Fori(1, PT) as t:
                for u in range(PH):
                    if u == 1:
                        ac.wait_ge(s["y_sum"], t + 2)
                        square_sum(sqj6, x2b, 128, 0, s["fin_ss"])
                    weights((u % 2, t * PH + (u + 2)))
            ac.wait_ge(s["y_sum"], PT + 2)
            square_sum(sqj6, x2b, 128, 0, s["fin_ss"])

        @block.vector
        def _(ve):
            def inv_rms(par, r):
                ms, root, y0, t, y1 = (rin[0:r, i:i + 1] for i in range(5))
                ve.tensor_scalar(ms, ss[0:r, par, 0:1], 1.0 / D, EPS, ALU.mult, ALU.add)
                ve.reciprocal(y0, ss[0:r, par, 1:2])
                ve.drain()
                ve.scalar_tensor_tensor(t, y0, y0, ms, ALU.mult, ALU.mult)
                ve.drain()
                ve.tensor_scalar(t, t, -0.5, 1.5, ALU.mult, ALU.add)
                ve.drain()
                ve.tensor_tensor(rinv[0:r, 1:2], y0, t, ALU.mult)
                ve.drain()

            ve.memset(tickv[:, :], 0.0)
            ve.memset(epsb[:, :], EPS)
            ve.drain().then_inc(s["ticked"], 1)
            ve.wait_ge(s["cexp_done"], 1)
            ve.tensor_scalar(cexp, cexp, 1.0, None, ALU.add)
            ve.drain()
            ve.reciprocal(cexp, cexp)
            ve.drain()
            ve.tensor_tensor(crow, crow, cexp, ALU.mult).then_inc(s["csil_done"], 1)
            ve.wait_ge(s["ct_ps"], 1)
            ve.tensor_copy(cw[:, :, :], PS[:, 0, 72:72 + 3 * CT].rearrange("p (j c) -> p j c", j=3))
            ve.tensor_copy(cT[:, :, :], PS[:, 0, 0:72].rearrange("p (k n) -> p k n", k=KT)).then_inc(s["ct_done"], 1)
            def add_bias(g):
                c = slice(g * 512, (g + 1) * 512)
                ve.wait_ge(s["pe_mod"], g + 1)
                ve.tensor_tensor(modrow[:, c], PS[0:9, 1 + g % 2, :], brow[:, c], ALU.add).then_inc(s["mod_ev"], 1)

            for g in range(6):
                add_bias(g)
            ve.wait_ge(s["vec1_ld"], 16 * (3 + 2 * TS))
            ve.scalar_tensor_tensor(A1, A1, 1.0, gmix, ALU.add, ALU.mult)
            ve.scalar_tensor_tensor(A1s, A1s, 1.0, gmix[0:NSAMP, :], ALU.add, ALU.mult)
            for t in range(TT):
                r = rows_of(t)
                x, h = xin[t % 2][0:r, :], hbuf[t % 2][0:r, :]
                A, B = (A1, B1) if t < PT else (A1s, B1s)
                ve.wait_ge(s["ss_done"], t + 1)
                inv_rms(t % 2, r)
                if t >= 2:
                    ve.wait_ge(s["pe_hT"], t - 1)
                ve.scalar_tensor_tensor(h, x, rinv[0:r, 1:2], A, ALU.mult, ALU.mult)
                ve.drain()
                ve.tensor_tensor(h, h, B, ALU.add).then_inc(s["h_done"], 1)
                if 1 <= t < 7:
                    add_bias(5 + t)
            ve.drain()
            ve.memset(uP[:, :, 0:2], 0.0)
            for c in range(CT):
                ct = 14 + c
                ve.wait_ge(s["p2_evA"], 14)
                ve.wait_ge(s["pe_p2"], ct + 1)
                for j in range(3):
                    b = 3 * (ct % 2) + j
                    w = min(TH, SEQ - j * TH)
                    last = ve.tensor_tensor(uP[:, c, 2 + j * TH:2 + j * TH + w], PS[:, b, 0:w], cgT[:, c, j * TH:j * TH + w], ALU.mult)
                    if w < TH:
                        last = ve.tensor_tensor(uS[:, c, :, 2:2 + TS], PS[:, b, w:TH].rearrange("p (n t) -> p n t", n=NS),
                                                cgT[:, c, SEQ:T].rearrange("p (n t) -> p n t", n=NS), ALU.mult)
                last.then_inc(s["p2_evD"], 1)
            ve.drain()
            for c in range(CT):
                ve.tensor_copy(utail[:, c, :].rearrange("p (n t) -> p n t", n=NS), uS[:, c, :, TS:TS + 2])
            for i in range(GRP):
                ve.tensor_copy(q16[:, :, i * TS:(i + 1) * TS], qT[:, i, SEQ:T].rearrange("p (n t) -> p n t", n=NS))
            for i in range(2):
                ve.wait_ge(s["pe_b"], i + 1)
                ve.tensor_copy(vnat[:, 4 * i:4 * i + 4, :], PS[:, 6 + i, :].rearrange("p (t c) -> p t c", t=4)).then_inc(s["b_ev"], 1)
            ve.wait_ge(s["pe_b"], 3)
            ve.tensor_copy(vnat[0:NSAMP, PT, :], PS[0:NSAMP, 0, 0:128])
            ve.tensor_copy(kn8, PS[0:NSAMP, 0, 128:256])
            ve.tensor_copy(kn7, PS[:, 0, 256:384]).then_inc(s["b_ev"], 1)
            ve.wait_ge(s["pe_b"], 4)
            for c in range(CT):
                last = ve.tensor_copy(uS[:, c, :, 0:2], PS[:, 1, c * 16:(c + 1) * 16].rearrange("p (n t) -> p n t", n=NS))
            last.then_inc(s["b_ev"], 1)
            for i in range(2):
                ve.wait_ge(s["pe_b"], 5 + i)
                ve.tensor_copy(cKT[:, 4 * i:4 * i + 4, :], PS[:, 4 + i, :].rearrange("p (t c) -> p t c", t=4)).then_inc(s["b_ev"], 1)
            ve.wait_ge(s["pe_b"], 7)
            ve.tensor_copy(utP, PS[0:2, 2, :]).then_inc(s["b_ev"], 1)
            ve.wait_ge(s["pe_b"], 8)
            ve.tensor_copy(utS, PS[0:16, 3, :]).then_inc(s["b_ev"], 1)

            ve.wait_ge(s["bias_ld"], 32)
            ve.wait_ge(s["table_ld"], 16 * NTAB)

            def soft1(n):
                par, kv, lo = n % 3, n % 2, 128 if n < 2 else 0
                ve.wait_ge(s["pe_sc"], n + 1)
                if n >= 3:
                    ve.wait_ge(s["pe_pt"], n - 2)
                ps = PS[:, 2 * kv:2 * kv + 2, :].rearrange("p b (i c) -> p (b i) c", i=2)
                ve.scalar_tensor_tensor(S[par][:, :, lo:256], ps[:, :, lo:256], DH ** -0.5,
                                        biasP[:, kv * GRP:(kv + 1) * GRP, lo:256], ALU.mult, ALU.add).then_inc(s["S_done"], 1)
                ve.drain()
                ve.tensor_reduce(mx[:, par, :], S[par][:, :, lo:256], AX.X, ALU.max)
                ve.drain()
                ve.tensor_tensor(mx[:, par, :], mx[:, par, :], sink[:, kv * GRP:(kv + 1) * GRP], ALU.max)
                ve.drain()
                ve.tensor_scalar(negm[:, par, :], mx[:, par, :], -1.0, None, ALU.mult)
                ve.tensor_tensor(esk[:, par, :], sink[:, kv * GRP:(kv + 1) * GRP], mx[:, par, :], ALU.subtract)
                ve.drain().then_inc(s["m_done"], 1)

            def soft2(n):
                par, lo = n % 3, 128 if n < 2 else 0
                ve.wait_ge(s["e_done"], n + 1)
                ve.tensor_tensor(rs[:, par, :], rs[:, par, :], esk[:, par, :], ALU.add)
                ve.drain()
                ve.reciprocal(rs[:, par, :], rs[:, par, :])
                ve.drain()
                ve.tensor_tensor(S[par][:, :, lo:256], S[par][:, :, lo:256],
                                 rs[:, par, :].unsqueeze(2).to_broadcast([128, GRP, 256 - lo]), ALU.mult).then_inc(s["p_done"], 1)

            soft1(0)
            soft1(1)
            for n in range(2 * PT):
                soft2(n)
                if n + 2 < 2 * PT:
                    soft1(n + 2)
            for kv in range(NKV):
                ve.wait_ge(s["pe_sc"], 2 * PT + kv + 1)
                ve.wait_ge(s["pe_pt"], 2 * PT)
                if kv:
                    ve.wait_ge(s["spt_ps"], 1)
                bs = biasS[:, kv, :].rearrange("p (n c) -> p n c", n=NS)
                ve.scalar_tensor_tensor(SS[:, :, 0:128], PS[0:16, 0:2, :].rearrange("p b (n c) -> p (b n) c", n=4), DH ** -0.5,
                                        bs[:, :, 0:128], ALU.mult, ALU.add)
                ve.scalar_tensor_tensor(SS[:, :, 128:160], PS[0:16, 2, 0:256].rearrange("p (n c) -> p n c", n=NS), DH ** -0.5,
                                        bs[:, :, 128:160], ALU.mult, ALU.add).then_inc(s["sss_done"], 1)
                ve.drain()
                ve.tensor_reduce(smx[:, :], SS, AX.X, ALU.max)
                ve.drain()
                ve.tensor_scalar(smx[:, :], smx[:, :], sinkS[:, kv:kv + 1], None, ALU.max)
                ve.drain()
                ve.tensor_tensor(SS, SS, smx[:, :].unsqueeze(2).to_broadcast([16, NS, 160]), ALU.subtract)
                ve.tensor_scalar(ses[:, :], smx[:, :], -1.0, sinkS[:, kv:kv + 1], ALU.mult, ALU.add)
                ve.drain().then_inc(s["sm_done"], 1)
                ve.wait_ge(s["se_done"], kv + 1)
                ve.tensor_reduce(sden[:, :], SS, AX.X, ALU.add)
                ve.drain()
                ve.tensor_tensor(sden[:, :], sden[:, :], ses[:, :], ALU.add)
                ve.drain()
                ve.reciprocal(sden[:, :], sden[:, :])
                ve.drain()
                ve.tensor_tensor(SS, SS, sden[:, :].unsqueeze(2).to_broadcast([16, NS, 160]), ALU.mult).then_inc(s["sp_done"], 1)

            ve.wait_ge(s["vec4_ld"], 16 * (4 + 3 * TS))
            ve.wait_ge(s["g1_ld"], 16 * (6 + 2 * NS))
            ve.scalar_tensor_tensor(vec[1], vec[1], 1.0, gffn, ALU.add, ALU.mult)
            ve.scalar_tensor_tensor(vecs[1], vecs[1], 1.0, gffn[0:NSAMP, :], ALU.add, ALU.mult)
            def residual(t):
                r, i, v = rows_of(t), t % 2, vec if t < PT else vecs
                x1 = x1b[i][0:r, :]
                ve.wait_ge(s["pe_o"], t + 1)
                if t >= 2:
                    ve.wait_ge(x1_st[i], 32 * (t // 2))
                ve.tensor_tensor(x1, PS[0:r, 2 * i:2 * i + 2, :].rearrange("p b c -> p (b c)"), v[0][0:r, :], ALU.mult)
                ve.wait_ge(x4_ld[i], 16 * (t // 2 + 1))
                ve.drain()
                ve.tensor_tensor(x1, x1, x4[i][0:r, :], ALU.add).then_inc(s["x1_done"], 1)

            def norm2(t):
                r, i, v = rows_of(t), t % 2, vec if t < PT else vecs
                h2 = h2b[i][0:r, :]
                ve.wait_ge(s["ss4_done"], t + 1)
                inv_rms(i, r)
                if t >= 2:
                    ve.wait_ge(s["pe_h2T"], t - 1)
                ve.scalar_tensor_tensor(h2, x1b[i][0:r, :], rinv[0:r, 1:2], v[1][0:r, :], ALU.mult, ALU.mult)
                ve.drain()
                ve.tensor_tensor(h2, h2, v[2][0:r, :], ALU.add).then_inc(s["h2_done"], 1)

            for t in range(TT):
                residual(t)
                norm2(t)
            ve.wait_ge(s["pe_k"], 1)
            ve.tensor_copy(keysT, PS[:, 0:4, :].rearrange("p b (k c) -> p (b k) c", k=4)).then_inc(s["k_ev"], 1)
            ve.wait_ge(s["pe_ss"], 1)
            for i in range(2):
                last = ve.tensor_copy(scb[i], PS[:, 5, i * 256:(i + 1) * 256].rearrange("p (a b) -> p a b", a=2))
            ve.drain()
            for i in range(2):
                ve.wait_ge(x1_st[i], 16 * (10 if i == 0 else 8))

            def top(m):
                idx, ahead = m
                par = idx % 2
                if not isinstance(ahead, int) or ahead > 0:
                    ve.wait_ge(s["sn_ev"], ahead)
                ve.memset(tickv[:, 0:1], 0.0)
                sc = scb[par]
                for p in range(2):
                    ve.max(topv[:, p, 0:8], sc[:, p, :])
                ve.drain()
                for p in range(2):
                    ve.max_index(topi[:, p, 0:8], topv[:, p, 0:8], sc[:, p, :])
                    ve.match_replace(sc2[:, p, :], topv[:, p, 0:8], sc[:, p, :], LOW)
                ve.drain()
                for p in range(2):
                    ve.max(topv[:, p, 8:16], sc2[:, p, :])
                ve.drain()
                for p in range(2):
                    ve.max_index(topi[:, p, 8:16], topv[:, p, 8:16], sc2[:, p, :])
                ve.tensor_tensor(cand, topv[:, 0, :].unsqueeze(2).to_broadcast([128, TOPK, TOPK]),
                                 topv[:, 1, :].unsqueeze(1).to_broadcast([128, TOPK, TOPK]), ALU.add)
                ve.drain()
                ve.tensor_copy(topf[:, :, :], topi[:, :, :])
                cf = cand.rearrange("p a b -> p (a b)")
                ve.max(best[:, par, 0:8], cf)
                ve.drain()
                ve.max_index(pos[:, 0:8], best[:, par, 0:8], cf)
                ve.match_replace(cand2, best[:, par, 0:8], cf, LOW)
                ve.tensor_scalar(nbest[:, par, :], best[:, par, 0:1], -1.0, None, ALU.mult)
                ve.drain()
                ve.max(best[:, par, 8:16], cand2)
                ve.drain()
                ve.max_index(pos[:, 8:16], best[:, par, 8:16], cand2)
                ve.drain()
                ve.tensor_scalar(posx[:, 0, :], pos[:, :], 4, None, ALU.logical_shift_right)
                ve.tensor_scalar(posx[:, 1, :], pos[:, :], 15, None, ALU.bitwise_and)
                ve.drain()
                ve.tensor_copy(posf[:, :, :], posx[:, :, :])
                ve.drain()
                for p, o in ((0, oh), (1, oh2)):
                    ve.tensor_tensor(o, iota[:, :].unsqueeze(1).to_broadcast([128, TOPK, TOPK]),
                                     posf[:, p, :].unsqueeze(2).to_broadcast([128, TOPK, TOPK]), ALU.is_equal)
                ve.drain()
                for p, o in ((0, oh), (1, oh2)):
                    ve.tensor_tensor(o, o, topf[:, p, :].unsqueeze(1).to_broadcast([128, TOPK, TOPK]), ALU.mult)
                ve.drain()
                for p, o in ((0, oh), (1, oh2)):
                    ve.tensor_reduce(ef[:, p, :], o, AX.X, ALU.add)
                ve.drain()
                ve.scalar_tensor_tensor(eid[idx][:, :], ef[:, 0, :], float(NK), ef[:, 1, :], ALU.mult, ALU.add).then_inc(s["idx_ready"], 1)

            def dots(m):
                par, mm_ = m
                for b in range(NB):
                    ve.wait_ge(u_ld[b % 2], mm_ * (32 * BATCH) + 16 * BATCH * (b // 2 + 1))
                    for k in range(b * BATCH, (b + 1) * BATCH):
                        last = ve.tensor_tensor_reduce(out=Ur[:, k % RING, :], in0=Ur[:, k % RING, :], in1=h2c, scale=1.0, scalar=0.0, op0=ALU.mult,
                                                       op1=ALU.add, accum_out=act[:, par, k:k + 1])
                    last.then_inc(s["dots_done"], 1)

            def weight(m):
                par, mm_ = m
                ve.wait_ge(s["exp_done"], mm_ + 1)
                ve.reciprocal(grec[:, par:par + 1], gsum[:, par:par + 1])
                ve.wait_ge(s["gelu_done"], mm_ + 1)
                ve.memset(tickv[:, 0:1], 0.0)
                ve.drain()
                ve.scalar_tensor_tensor(wgt[:, par, :], gex[:, par, :], grec[:, par:par + 1], gel[:, par, :],
                                        ALU.mult, ALU.mult).then_inc(s["w_ready"], 1)

            def gather_sum(m, first):
                par, mm_ = m
                ve.wait_ge(s["pv_done"], mm_ * NB + NB)
                ps = PS[:, 2 * par:2 * par + 2, :].rearrange("p b c -> p (b c)")
                if first:
                    ve.tensor_copy(Y, ps).then_inc(s["y_added"], 1)
                else:
                    ve.tensor_tensor(Y, Y, ps, ALU.add).then_inc(s["y_added"], 1)

            def final_sample():
                ve.drain().then_inc(s["y_sum"], 1)
                ve.wait_ge(s["pe_sel"], 1)
                ve.wait_ge(s["vec6_ld"], 16 * (2 + TS))
                ve.tensor_tensor(x2b[0:NSAMP, :], PS[0:NSAMP, 4:6, :].rearrange("p b c -> p (b c)"), g2s, ALU.mult)
                ve.wait_ge(s["x1_ld"], 16)
                ve.drain()
                ve.tensor_tensor(x2b[0:NSAMP, :], x2b[0:NSAMP, :], x1c[0:NSAMP, :], ALU.add).then_inc(s["y_sum"], 1)
                ve.wait_ge(s["fin_ss"], 1)
                inv_rms(0, NSAMP)
                ve.scalar_tensor_tensor(yb[0:NSAMP, :], x2b[0:NSAMP, :], rinv[0:NSAMP, 1:2], gfv[0:NSAMP, :], ALU.mult,
                                        ALU.mult).then_inc(s["y_out"], 1)

            def final(t):
                ve.drain()
                ve.tensor_tensor(x2b, Y, g2v, ALU.mult)
                ve.wait_ge(s["x1_ld"], t * 16 + 16)
                ve.memset(tickv[:, 0:1], 0.0)
                ve.drain()
                ve.tensor_tensor(x2b, x2b, x1c, ALU.add).then_inc(s["y_sum"], 1)
                ve.wait_ge(s["fin_ss"], t + 1)
                inv_rms(0, 128)
                ve.wait_ge(s["out_st"], t * 16)
                ve.scalar_tensor_tensor(yb, x2b, rinv[:, 1:2], gfv, ALU.mult, ALU.mult).then_inc(s["y_out"], 1)

            def units(t):
                for u in range(PH):
                    m = (u % 2, t * PH + (u + 2))
                    top(((u + 3) % 4, t * PH + (u + 2)))
                    gather_sum((u % 2, t * PH + u), u == 2 or (u == 0 and isinstance(t, int)))
                    if u == 0:
                        ve.wait_ge(s["h2_ld"], t * 16 + 16)
                        ve.memset(tickv[:, 0:1], 0.0)
                    if u == 1:
                        if isinstance(t, int):
                            final_sample()
                        else:
                            final(t)
                    dots(m)
                    weight(m)

            top((0, 0))
            top((1, 0))
            ve.wait_ge(s["h2s_ld"], 64)
            dots((0, 0))
            weight((0, 0))
            top((2, 1))
            dots((1, 1))
            weight((1, 1))
            units(0)
            with ve.Fori(1, PT) as t:
                units(t)
            for m in (UNITS - 2, UNITS - 1):
                ve.drain()
                gather_sum((m % 2, m), False)
            final(PT)


def constants():
    slopes = [2.0 ** -(h + 1) for h in range(NH)]
    d = np.arange(128)[:, None] + 128 - np.arange(256)[None, :]
    ok = (d >= 0) & (d < WIN)
    alibi_p = np.stack([np.where(ok, -sl * d, NEG) for sl in slopes], 1).astype(np.float32)
    alibi_s = np.full((16, NKV, NS, 160), NEG, np.float32)
    for kv in range(NKV):
        for i in range(GRP):
            for t in range(TS):
                for n in range(NS):
                    sl, row = slopes[kv * GRP + i], i * TS + t
                    for key in range(128 + TS):
                        dist = 128 + t - key
                        if 0 <= dist < WIN:
                            alibi_s[row, kv, n, key if key < 128 else 128 + n * TS + key - 128] = -sl * dist
    return {"ident": np.eye(128, dtype=np.float32), "sel": np.tile(np.eye(NSAMP, dtype=np.float32), (4, 1)),
            "iota": np.tile(np.arange(TOPK, dtype=np.float32), (128, 1)), "alibi_p": alibi_p,
            "alibi_s": alibi_s.reshape(16, NKV, NS * 160)}


_SHAPES = {
    "x_prompt": (SEQ, D), "x_sample": (NSAMP, D), "c_prompt": (1, D), "c_sample": (NS, D), "cache_k": (NS, WIN, 128),
    "cache_v": (NS, WIN, 128), "state_conv": (2 * NS, DC), "norm_mix_g": (D,), "norm_ffn_g": (D,), "w_ada": (D, NADA * D),
    "b_ada": (NADA * D,), "w_in": (D, INC), "conv_w": (3, DC), "attn_sinks": (NH,), "w_out": (D, D),
    "peer_wq": (D, PH * 256), "peer_keys": (PH, 2, NK, 128), "peer_u": (NK * NK, D), "peer_v": (NK * NK, D),
    "norm_final_g": (D,),
}
_OUTS = {
    "y_prompt": ((SEQ, D), (1, SEQ, D)), "y_sample": ((NSAMP, D), (NS, TS, D)),
    "k_prompt": ((128, 128), (1, 1, WIN, NKV, DH)), "v_prompt": ((128, 128), (1, 1, WIN, NKV, DH)),
    "conv_prompt": ((2, DC), (1, 1, 2, DC)), "k_sample": ((NS, WIN, 128), (1, NS, WIN, NKV, DH)),
    "v_sample": ((NS, WIN, 128), (1, NS, WIN, NKV, DH)), "conv_sample": ((2 * NS, DC), (1, NS, 2, DC)),
}


def kernel(**inputs):
    import numpy as _np
    import concourse.bacc as _bacc
    from concourse import mybir as _mybir
    from concourse.bass_utils import run_bass_kernel_spmd as _run

    nc = _bacc.Bacc("TRN2", target_bir_lowering=False, num_devices=1)
    arrays = {f"in_{n}": _np.ascontiguousarray(inputs[n]).reshape(shape) for n, shape in _SHAPES.items()}
    arrays |= {f"in_{n}": v for n, v in constants().items()}
    a = {n[3:]: nc.dram_tensor(n, v.shape, _mybir.dt.from_np(v.dtype), kind="ExternalInput").ap() for n, v in arrays.items()}
    out = {n: nc.dram_tensor(f"out_{n}", shape, _mybir.dt.float32, kind="ExternalOutput").ap() for n, (shape, _) in _OUTS.items()}
    build(nc, a, out)
    r = _run(nc, [arrays], core_ids=[0])
    return tuple(r.results[0][f"out_{n}"].reshape(full) for n, (_, full) in _OUTS.items())
```
